# Optimizing a Trainium2 kernel written in Bass

```python
import math
import jax, jax.numpy as jnp
from jax import lax
import numpy as np

D_MODEL = 1024
BATCH = 1
SEQ = 512
DEPTH = 2

GRID_W = 64
CTX_LEN = 256
EPS = 1e-6
NEG_INF = -1e30

NA_HEADS = 8
NA_HEAD_DIM = 64
NA_WIDTH = NA_HEADS * NA_HEAD_DIM
NA_WIN_ROWS = 8
NA_WIN_COLS = 16
NA_COL_BLOCK = 16
NA_KEY_COLS = 32
SG_GROUPS = 4
SG_GROUP_DIM = 128
SG_WIDTH = SG_GROUPS * SG_GROUP_DIM
SG_CHUNK = 128
MLA_HEADS = 8
MLA_Q_RANK = 256
MLA_KV_RANK = 128
MLA_NOPE_DIM = 64
MLA_ROPE_DIM = 32
MLA_V_DIM = 64
MLA_QK_DIM = MLA_NOPE_DIM + MLA_ROPE_DIM
MLA_BLOCK = 128
ROPE_BASE = 10000.0
N_BRANCHES = 3
BRANCH_WIDTH = 512
PEER_HEADS = 8
PEER_KEYS = 128
PEER_EXPERTS = PEER_KEYS * PEER_KEYS
PEER_QUERY_DIM = 256
PEER_HALF = PEER_QUERY_DIM // 2
PEER_TOPK = 16
PEER_TOKEN_BLOCK = 128

IN_SPLITS = (
    NA_WIDTH,
    2 * NA_WIDTH,
    3 * NA_WIDTH,
    3 * NA_WIDTH + MLA_Q_RANK,
    3 * NA_WIDTH + MLA_Q_RANK + MLA_KV_RANK,
    3 * NA_WIDTH + MLA_Q_RANK + MLA_KV_RANK + MLA_ROPE_DIM,
    3 * NA_WIDTH + MLA_Q_RANK + MLA_KV_RANK + MLA_ROPE_DIM + 2 * SG_WIDTH,
)
IN_COLS = 3 * NA_WIDTH + MLA_Q_RANK + MLA_KV_RANK + MLA_ROPE_DIM + 2 * SG_WIDTH + N_BRANCHES * D_MODEL

kernel_name = "hybrid_na_sgmlp_mla_peer_diffusion_block"

def rms_norm(x, g):
    xf = x.astype(jnp.float32)
    y = xf * lax.rsqrt(jnp.mean(xf * xf, axis=-1, keepdims=True) + EPS)
    return (y * g.astype(jnp.float32)).astype(x.dtype)

def modulate(h, shift, scale):
    return h * (1.0 + scale) + shift

def split_heads(x, n):
    return x.reshape(x.shape[:-1] + (n, x.shape[-1] // n))

def axial_rope_tables(length, dtype):
    t = jnp.arange(length)
    row = (t // GRID_W).astype(jnp.float32)
    col = (t % GRID_W).astype(jnp.float32)
    n_freq = MLA_ROPE_DIM // 4
    inv_freq = ROPE_BASE ** (-jnp.arange(n_freq, dtype=jnp.float32) / n_freq)
    ang = jnp.concatenate([row[:, None] * inv_freq, col[:, None] * inv_freq], axis=-1)
    return jnp.cos(ang).astype(dtype), jnp.sin(ang).astype(dtype)

def apply_rope(x, cos, sin):
    x1, x2 = jnp.split(x, 2, axis=-1)
    return jnp.concatenate([x1 * cos - x2 * sin, x1 * sin + x2 * cos], axis=-1)

def dense_softmax_attention(q, k, v):
    s = jnp.einsum('bqhd,bkhd->bhqk', q, k, preferred_element_type=jnp.float32) * (q.shape[-1] ** -0.5)
    p = jax.nn.softmax(s, axis=-1).astype(v.dtype)
    return jnp.einsum('bhqk,bkhd->bqhd', p, v)

def na_column_blocks():
    n_blk = GRID_W // NA_COL_BLOCK
    qc = np.arange(GRID_W).reshape(n_blk, NA_COL_BLOCK)
    win_start = np.clip(qc - NA_WIN_COLS // 2, 0, GRID_W - NA_WIN_COLS)
    blk_start = np.clip(np.arange(n_blk) * NA_COL_BLOCK - NA_WIN_COLS // 2, 0, GRID_W - NA_KEY_COLS)
    kc = blk_start[:, None] + np.arange(NA_KEY_COLS)
    valid = (kc[:, None, :] >= win_start[:, :, None]) & (kc[:, None, :] < win_start[:, :, None] + NA_WIN_COLS)
    col_idx = np.clip(kc[:, None, :] - qc[:, :, None] + NA_WIN_COLS - 1, 0, 2 * NA_WIN_COLS - 2)
    return kc, valid, col_idx

def neighbourhood_attention(q, k, v, k_ctx, v_ctx, rpb):
    B, S, H, d = q.shape
    rows = S // GRID_W
    wr = min(NA_WIN_ROWS, rows)
    n_blk = GRID_W // NA_COL_BLOCK
    kcols, valid, col_idx = na_column_blocks()
    scale = d ** -0.5
    kg = k.reshape(B, rows, GRID_W, H, d)
    vg = v.reshape(B, rows, GRID_W, H, d)
    qg = jnp.moveaxis(q.reshape(B, rows, n_blk, NA_COL_BLOCK, H, d), 1, 0)
    n_loc = wr * NA_KEY_COLS

    def row_fn(args):
        r, qr = args
        rs = jnp.clip(r - wr // 2, 0, rows - wr)
        kr = lax.dynamic_slice_in_dim(kg, rs, wr, axis=1)[:, :, kcols]
        vr = lax.dynamic_slice_in_dim(vg, rs, wr, axis=1)[:, :, kcols]
        s_loc = jnp.einsum('bnqhd,binkhd->bhnqik', qr, kr, preferred_element_type=jnp.float32) * scale
        row_off = rs + jnp.arange(wr) - r + NA_WIN_ROWS - 1
        bias = jnp.transpose(rpb[:, row_off][:, :, col_idx], (0, 2, 3, 1, 4))
        s_loc = jnp.where(valid[:, :, None, :], s_loc + bias.astype(jnp.float32), NEG_INF)
        s_ctx = jnp.einsum('bnqhd,bchd->bhnqc', qr, k_ctx, preferred_element_type=jnp.float32) * scale
        s = jnp.concatenate([s_loc.reshape(B, H, n_blk, NA_COL_BLOCK, n_loc), s_ctx], axis=-1)
        p = jax.nn.softmax(s, axis=-1).astype(v.dtype)
        p_loc = p[..., :n_loc].reshape(B, H, n_blk, NA_COL_BLOCK, wr, NA_KEY_COLS)
        return (jnp.einsum('bhnqik,binkhd->bnqhd', p_loc, vr)
                + jnp.einsum('bhnqc,bchd->bnqhd', p[..., n_loc:], v_ctx))

    out = lax.map(row_fn, (jnp.arange(rows), qg))
    return jnp.moveaxis(out, 0, 1).reshape(B, S, H * d)

def spatial_gating(uv, g_sg, w_s, b_s):
    B, L, _ = uv.shape
    u, v = jnp.split(jax.nn.gelu(uv), 2, axis=-1)
    v = rms_norm(v, g_sg).reshape(B, L // SG_CHUNK, SG_CHUNK, SG_GROUPS, SG_GROUP_DIM)
    v = jnp.einsum('gpq,bnqgc->bnpgc', w_s, v) + b_s.T[:, :, None]
    return u * v.reshape(B, L, SG_WIDTH)

def mla_queries(cq, lp):
    q = split_heads(rms_norm(cq, lp['mla_g_cq']) @ lp['mla_w_uq'], MLA_HEADS)
    qn = rms_norm(q[..., :MLA_NOPE_DIM], lp['mla_g_qn'])
    qr = rms_norm(q[..., MLA_NOPE_DIM:], lp['mla_g_qr'])
    return qn, qr

def mla_keys(ckv, kr, lp):
    kv = rms_norm(ckv, lp['mla_g_ckv'])
    kn = rms_norm(split_heads(kv @ lp['mla_w_uk'], MLA_HEADS), lp['mla_g_kn'])
    v = split_heads(kv @ lp['mla_w_uv'], MLA_HEADS)
    return kn, rms_norm(kr, lp['mla_g_kr']), v

def mla_attend(qn, qr, kn, kr, v):
    s = (jnp.einsum('bqhd,bkhd->bhqk', qn, kn, preferred_element_type=jnp.float32)
         + jnp.einsum('bqhd,bkd->bhqk', qr, kr, preferred_element_type=jnp.float32))
    p = jax.nn.softmax(s * (MLA_QK_DIM ** -0.5), axis=-1).astype(v.dtype)
    return jnp.einsum('bhqk,bkhd->bqhd', p, v)

def mla_latent(qn, qr, kn, kr, v):
    B, S, H, _ = qn.shape
    nb = S // MLA_BLOCK
    qn_b = jnp.moveaxis(qn.reshape(B, nb, MLA_BLOCK, H, MLA_NOPE_DIM), 1, 0)
    qr_b = jnp.moveaxis(qr.reshape(B, nb, MLA_BLOCK, H, MLA_ROPE_DIM), 1, 0)
    out = lax.map(lambda a: mla_attend(a[0], a[1], kn, kr, v), (qn_b, qr_b))
    return jnp.moveaxis(out, 0, 1).reshape(B, S, H * MLA_V_DIM)

def branch_merge(a, s, m, gate_logits, w_branch, w_out):
    g_a, g_s, g_m = jnp.split(jax.nn.sigmoid(gate_logits), N_BRANCHES, axis=-1)
    merged = g_a * (a @ w_branch[0]) + g_s * (s @ w_branch[1]) + g_m * (m @ w_branch[2])
    return merged @ w_out

def peer_ffn(h, w_q, sub_k1, sub_k2, exp_u, exp_v):
    B, L, D = h.shape
    tok = h.reshape(-1, PEER_TOKEN_BLOCK, D)

    def block(hb):
        q1, q2 = jnp.split(split_heads(hb @ w_q, PEER_HEADS), 2, axis=-1)
        s1 = jnp.einsum('thd,kd->thk', q1, sub_k1, preferred_element_type=jnp.float32)
        s2 = jnp.einsum('thd,kd->thk', q2, sub_k2, preferred_element_type=jnp.float32)
        v1, i1 = lax.top_k(s1, PEER_TOPK)
        v2, i2 = lax.top_k(s2, PEER_TOPK)
        cand_s = (v1[..., :, None] + v2[..., None, :]).reshape(hb.shape[0], PEER_HEADS, PEER_TOPK * PEER_TOPK)
        cand_i = (i1[..., :, None] * PEER_KEYS + i2[..., None, :]).reshape(hb.shape[0], PEER_HEADS, PEER_TOPK * PEER_TOPK)
        best_s, pos = lax.top_k(cand_s, PEER_TOPK)
        idx = jnp.take_along_axis(cand_i, pos, axis=-1)
        gate = jax.nn.softmax(best_s, axis=-1).astype(hb.dtype)
        act = jax.nn.gelu(jnp.einsum('thkd,td->thk', exp_u[idx], hb))
        return jnp.einsum('thk,thkd->td', gate * act, exp_v[idx])

    return lax.map(block, tok).reshape(B, L, D)

def trunk_layer(xc, xl, c, c_ctx, cos, sin, lp, last):
    B, C, _ = xc.shape
    mod_l = jnp.split((jax.nn.silu(c) @ lp['w_mod'] + lp['b_mod'])[:, None, :], 6, axis=-1)
    mod_c = jnp.split((jax.nn.silu(c_ctx) @ lp['w_mod'] + lp['b_mod'])[None, None, :], 6, axis=-1)

    hl = modulate(rms_norm(xl, lp['g_norm1']), mod_l[0], mod_l[1])
    hc = modulate(rms_norm(xc, lp['g_norm1']), mod_c[0], mod_c[1])
    naq_l, nak_l, nav_l, cq_l, ckv_l, kr_l, uv_l, gate_l = jnp.split(hl @ lp['w_in'], IN_SPLITS, axis=-1)
    naq_c, nak_c, nav_c, cq_c, ckv_c, kr_c, uv_c, gate_c = jnp.split(hc @ lp['w_in'], IN_SPLITS, axis=-1)

    ka_c = rms_norm(split_heads(nak_c, NA_HEADS), lp['na_g_k'])
    va_c = split_heads(nav_c, NA_HEADS)
    a_l = neighbourhood_attention(rms_norm(split_heads(naq_l, NA_HEADS), lp['na_g_q']),
                                  rms_norm(split_heads(nak_l, NA_HEADS), lp['na_g_k']),
                                  split_heads(nav_l, NA_HEADS), ka_c, va_c, lp['na_rpb'])
    qn_l, qr_l = mla_queries(cq_l, lp)
    qr_l = apply_rope(qr_l, cos[:, None, :], sin[:, None, :])
    kn_l, krr_l, vm_l = mla_keys(ckv_l, kr_l, lp)
    krr_l = apply_rope(krr_l, cos, sin)
    kn_c, krr_c, vm_c = mla_keys(ckv_c, kr_c, lp)
    m_l = mla_latent(qn_l, qr_l,
                     jnp.concatenate([kn_c, kn_l], axis=1),
                     jnp.concatenate([krr_c, krr_l], axis=1),
                     jnp.concatenate([vm_c, vm_l], axis=1))
    s_l = spatial_gating(uv_l, lp['sg_g'], lp['sg_w'], lp['sg_b'])
    xl_new = xl + mod_l[2] * branch_merge(a_l, s_l, m_l, gate_l, lp['w_branch'], lp['w_out'])

    if not last:
        a_c = dense_softmax_attention(rms_norm(split_heads(naq_c, NA_HEADS), lp['na_g_q']), ka_c, va_c)
        qn_c, qr_c = mla_queries(cq_c, lp)
        m_c = mla_attend(qn_c, qr_c, kn_c, krr_c, vm_c)
        s_c = spatial_gating(uv_c, lp['sg_g'], lp['sg_w'], lp['sg_b'])
        xc = xc + mod_c[2] * branch_merge(a_c.reshape(B, C, NA_WIDTH), s_c, m_c.reshape(B, C, MLA_HEADS * MLA_V_DIM),
                                          gate_c, lp['w_branch'], lp['w_out'])

    h2 = modulate(rms_norm(xl_new, lp['g_norm2']), mod_l[3], mod_l[4])
    xl_new = xl_new + mod_l[5] * peer_ffn(h2, lp['peer_w_q'], lp['peer_k1'], lp['peer_k2'], lp['peer_u'], lp['peer_v'])
    if not last:
        h2c = modulate(rms_norm(xc, lp['g_norm2']), mod_c[3], mod_c[4])
        xc = xc + mod_c[5] * peer_ffn(h2c, lp['peer_w_q'], lp['peer_k1'], lp['peer_k2'], lp['peer_u'], lp['peer_v'])
    return xc, xl_new

def setup_inputs(seed: int = 0) -> dict:
    key = jax.random.key(seed)
    ks = iter(jax.random.split(key, 40))

    def nrm(shape, std):
        return jax.random.normal(next(ks), shape, jnp.float32) * std

    def gain(shape):
        return 1.0 + nrm(shape, 0.02)

    L, D = DEPTH, D_MODEL
    return {
        'x': nrm((BATCH, SEQ, D), 1.0),
        'c': nrm((BATCH, D), 1.0),
        'ctx': nrm((BATCH, CTX_LEN, D), 1.0),
        'c_ctx': nrm((D,), 1.0),
        'w_mod': nrm((L, D, 6 * D), 0.5 * D ** -0.5),
        'b_mod': nrm((L, 6 * D), 0.02),
        'g_norm1': gain((L, D)),
        'w_in': nrm((L, D, IN_COLS), D ** -0.5),
        'na_g_q': gain((L, NA_HEAD_DIM)),
        'na_g_k': gain((L, NA_HEAD_DIM)),
        'na_rpb': nrm((L, NA_HEADS, 2 * NA_WIN_ROWS - 1, 2 * NA_WIN_COLS - 1), 0.1),
        'sg_g': gain((L, SG_WIDTH)),
        'sg_w': nrm((L, SG_GROUPS, SG_CHUNK, SG_CHUNK), SG_CHUNK ** -0.5),
        'sg_b': nrm((L, SG_GROUPS, SG_CHUNK), 0.02),
        'mla_g_cq': gain((L, MLA_Q_RANK)),
        'mla_w_uq': nrm((L, MLA_Q_RANK, MLA_HEADS * MLA_QK_DIM), MLA_Q_RANK ** -0.5),
        'mla_g_ckv': gain((L, MLA_KV_RANK)),
        'mla_w_uk': nrm((L, MLA_KV_RANK, MLA_HEADS * MLA_NOPE_DIM), MLA_KV_RANK ** -0.5),
        'mla_w_uv': nrm((L, MLA_KV_RANK, MLA_HEADS * MLA_V_DIM), MLA_KV_RANK ** -0.5),
        'mla_g_qn': gain((L, MLA_NOPE_DIM)),
        'mla_g_qr': gain((L, MLA_ROPE_DIM)),
        'mla_g_kn': gain((L, MLA_NOPE_DIM)),
        'mla_g_kr': gain((L, MLA_ROPE_DIM)),
        'w_branch': nrm((L, N_BRANCHES, BRANCH_WIDTH, D), BRANCH_WIDTH ** -0.5),
        'w_out': nrm((L, D, D), D ** -0.5),
        'g_norm2': gain((L, D)),
        'peer_w_q': nrm((L, D, PEER_HEADS * PEER_QUERY_DIM), D ** -0.5),
        'peer_k1': nrm((L, PEER_KEYS, PEER_HALF), PEER_HALF ** -0.5),
        'peer_k2': nrm((L, PEER_KEYS, PEER_HALF), PEER_HALF ** -0.5),
        'peer_u': nrm((L, PEER_EXPERTS, D), D ** -0.5),
        'peer_v': nrm((L, PEER_EXPERTS, D), PEER_HEADS ** -0.5),
    }

def reference(x, c, ctx, c_ctx, w_mod, b_mod, g_norm1, w_in, na_g_q, na_g_k, na_rpb, sg_g, sg_w, sg_b,
              mla_g_cq, mla_w_uq, mla_g_ckv, mla_w_uk, mla_w_uv, mla_g_qn, mla_g_qr, mla_g_kn, mla_g_kr,
              w_branch, w_out, g_norm2, peer_w_q, peer_k1, peer_k2, peer_u, peer_v):
    cos, sin = axial_rope_tables(x.shape[1], x.dtype)
    xc, xl = ctx, x
    for l in range(DEPTH):
        lp = {
            'w_mod': w_mod[l], 'b_mod': b_mod[l], 'g_norm1': g_norm1[l], 'w_in': w_in[l],
            'na_g_q': na_g_q[l], 'na_g_k': na_g_k[l], 'na_rpb': na_rpb[l],
            'sg_g': sg_g[l], 'sg_w': sg_w[l], 'sg_b': sg_b[l],
            'mla_g_cq': mla_g_cq[l], 'mla_w_uq': mla_w_uq[l], 'mla_g_ckv': mla_g_ckv[l],
            'mla_w_uk': mla_w_uk[l], 'mla_w_uv': mla_w_uv[l], 'mla_g_qn': mla_g_qn[l],
            'mla_g_qr': mla_g_qr[l], 'mla_g_kn': mla_g_kn[l], 'mla_g_kr': mla_g_kr[l],
            'w_branch': w_branch[l], 'w_out': w_out[l], 'g_norm2': g_norm2[l],
            'peer_w_q': peer_w_q[l], 'peer_k1': peer_k1[l], 'peer_k2': peer_k2[l],
            'peer_u': peer_u[l], 'peer_v': peer_v[l],
        }
        xc, xl = trunk_layer(xc, xl, c, c_ctx, cos, sin, lp, l == DEPTH - 1)
    return xl


_drawn_inputs = setup_inputs


def setup_inputs(seed=0):
    import zlib

    import numpy as np

    out = dict(_drawn_inputs(seed))
    spreads = {}
    factors = {'ctx': 2.696,
     'g_norm1': 7.123,
     'na_g_q': 8.0,
     'na_g_k': 8.0,
     'na_rpb': 8.0,
     'sg_g': 8.0,
     'sg_b': 8.0,
     'mla_g_cq': 8.0,
     'mla_g_ckv': 8.0,
     'mla_g_qn': 8.0,
     'mla_g_qr': 8.0,
     'mla_g_kn': 8.0,
     'mla_g_kr': 8.0,
     'g_norm2': 23.125}
    for name, (base, spread) in spreads.items():
        noise = np.random.default_rng([zlib.crc32(name.encode()), seed]).standard_normal(out[name].shape)
        drawn = base * np.exp(spread * noise) if base else spread * noise
        out[name] = __import__('jax').numpy.asarray(drawn.astype(out[name].dtype))
    for name, factor in factors.items():
        out[name] = (out[name] * factor).astype(out[name].dtype)
    return out
```

```python
import concourse.bass as bass
from concourse import mybir
from contextlib import ExitStack
import numpy as np

P = 128
D, SEQ, CTX, LAYERS = 1024, 512, 256, 2
T = CTX + SEQ
DK = D // P
EPS = 1e-6
GRID_W, ROWS = 64, SEQ // 64
HEADS, HD = 8, 64
NA_W = HEADS * HD
WIN_R, WIN_C, KEY_COLS, COL_BLK = 8, 16, 32, 16
NBLK = GRID_W // COL_BLK
NLOC = ROWS * KEY_COLS
Q_RANK, KV_RANK, ROPE, QK = 256, 128, 32, 96
SG_W, GROUPS = 512, 4
C_Q, C_K, C_V = 0, NA_W, 2 * NA_W
C_CQ = 3 * NA_W
C_CKV = C_CQ + Q_RANK
C_U = C_CKV + KV_RANK + ROPE
C_SV = C_U + SG_W
C_GATE = C_SV + SG_W
PH, PK, TOPK, NEXP = 8, 128, 16, 128 * 128
RO, CO = 2 * WIN_R - 1, 2 * WIN_C - 1
NBIAS = HEADS * RO * CO
BIAS_SHIFT = [15, 7, -1]
KIND = [0, 1, 1, 2]
PAD = 16
W_SLOTS, W_LEN = 4, 2048
NEG = -3.0e38
U_RING, V_RING = 8, 4
IDX_RING = 4


def constants():
    f = np.float32
    ident = np.eye(P, dtype=f)
    ones = np.full((P, P), 1.0 / D, f)
    blk = np.zeros((P, P), f)
    blk[:64, :64] = blk[64:, 64:] = 1.0 / 64
    blkq = np.zeros((P, P), f)
    blkq[:64, :64] = 1.0 / 64
    blkq[64:96, 64:96] = 1.0 / 32
    rot = np.zeros((P, P), f)
    for j in range(16):
        rot[80 + j, 64 + j] = -1.0
        rot[64 + j, 80 + j] = 1.0
    t = np.arange(SEQ)
    nf = ROPE // 4
    inv = (np.float32(10000.0) ** (-np.arange(nf, dtype=f) / np.float32(nf))).astype(f)
    ang = np.concatenate([(t // GRID_W).astype(f)[:, None] * inv, (t % GRID_W).astype(f)[:, None] * inv], -1)
    cs = np.zeros((P, 2, SEQ), f)
    for a in (64, 80):
        cs[a:a + 16, 0] = np.cos(ang).T
        cs[a:a + 16, 1] = np.sin(ang).T
    mask = np.zeros((P, 3, ROWS, KEY_COLS), f)
    for kind, blkno in ((0, 0), (1, 1), (2, 3)):
        start = min(max(blkno * COL_BLK - WIN_C // 2, 0), GRID_W - KEY_COLS)
        for i in range(COL_BLK):
            qc = blkno * COL_BLK + i
            ws = min(max(qc - WIN_C // 2, 0), GRID_W - WIN_C)
            bad = [j for j in range(KEY_COLS) if not ws <= start + j < ws + WIN_C]
            for r in range(ROWS):
                mask[r * COL_BLK + i, kind][:, bad] = -1e30
    iota = np.tile(np.arange(16, dtype=f)[None, None, :], (P, 16, 1))
    return np.concatenate([ident, ones, blk, blkq, rot, cs.reshape(P, -1), mask.reshape(P, -1),
                           iota.reshape(P, -1)], axis=1)


N_CONST = 5 * P + 2 * SEQ + 3 * NLOC + 256


def program(nc, x, ctx_in, w_mod, w_in, na_rpb, sg_w, sg_b, mla_w_uq, mla_w_uk, mla_w_uv, w_branch, w_out, peer_w_q,
            peer_k1, peer_k2, peer_u, peer_v, cond, columns, const, out):
    F, U32 = mybir.dt.float32, mybir.dt.uint32
    ALU, ACT, AX = mybir.AluOpType, mybir.ActivationFunctionType, mybir.AxisListType
    u_rows = peer_u.rearrange("l e d -> (l e) d")
    v_rows = peer_v.rearrange("l e d -> (l e) d")

    rpb_pad = nc.dram_tensor("rpb_pad", [LAYERS * NBIAS + 2 * PAD], F, kind="Internal").ap()
    rpb_rows = nc.dram_tensor("rpb_rows", [LAYERS, HEADS, 3, COL_BLK, RO * KEY_COLS], F, kind="Internal").ap()

    with ExitStack() as stack:
        def sb(name, shape, dt=F):
            return stack.enter_context(nc.sbuf_tensor(name, shape, dt))

        def sem(name):
            return stack.enter_context(nc.semaphore(name))

        X = sb("X", [P, DK, T])
        consts = sb("consts", [P, N_CONST])
        o = 0
        ident = consts[:, 0:P]
        ones = consts[:, P:2 * P]
        blk64 = consts[:, 2 * P:3 * P]
        blkq = consts[:, 3 * P:4 * P]
        rot = consts[:, 4 * P:5 * P]
        o = 5 * P
        cosT = consts[:, o:o + SEQ]
        sinT = consts[:, o + SEQ:o + 2 * SEQ]
        o += 2 * SEQ
        masks = consts[:, o:o + 3 * NLOC]
        o += 3 * NLOC
        iota16 = consts[:, o:o + 256].rearrange("p (k j) -> p k j", k=16)

        modraw = sb("modraw", [P, 48])
        modc = sb("modc", [P, 48, 2])
        gains = sb("gains", [P, 32])
        G_N1, G_N2, G_Q, G_K, G_SG, G_CQ, G_CKV, G_QQ, G_KN, G_KR = 0, 8, 16, 17, 18, 22, 24, 25, 26, 27
        gs1 = sb("gs1", [P, 2, DK])
        gs2 = sb("gs2", [P, 2, DK])
        epsc = sb("epsc", [P, 1])
        cT = sb("cT", [P, DK, 2])
        cS = sb("cS", [P, DK, 2])
        stats = sb("stats", [P, 4, 8])
        g2t = sb("g2t", [P, 6, DK])
        idx = sb("idx", [P, IDX_RING, TOPK], U32)
        gate = sb("gate", [P, IDX_RING, TOPK])
        dots = sb("dots", [P, 2, TOPK])
        gel = sb("gel", [P, 2, TOPK])
        wgt = sb("wgt", [P, 2, TOPK])

        wring = sb("wring", [P, W_SLOTS, W_LEN])
        R_LEN = 35600
        region = sb("region", [P, R_LEN])

        def at(off, n):
            assert off + n <= R_LEN
            return region[:, off:off + n]

        hT = at(0, DK * T).rearrange("p (k t) -> p k t", k=DK)
        R1 = DK * T
        R1_LEN = 13312
        naq = at(R1, 3072).rearrange("p (c t) -> p c t", c=4)
        nak = at(R1 + 3072, 3072).rearrange("p (c t) -> p c t", c=4)
        vna = at(R1 + 6144, 3072).rearrange("p (t f) -> p t f", t=6)
        vblk = at(R1 + 9216, 4096).rearrange("p (n c f) -> p n c f", n=NBLK, c=2)
        cqT = at(R1, 1536).rearrange("p (c t) -> p c t", c=2)
        ckvT = at(R1 + 1536, T)
        krT = at(R1 + 2304, T)
        vm = at(R1 + 3072, 3072).rearrange("p (t f) -> p t f", t=6)
        qm = at(R1 + 6144, 3072).rearrange("p (h t) -> p h t", h=4)
        km = at(R1 + 9216, 3072).rearrange("p (h t) -> p h t", h=4)
        uT = at(R1, 3072).rearrange("p (c t) -> p c t", c=4)
        vg = at(R1 + 3072, 3072).rearrange("p (t f) -> p t f", t=6)
        wsT = at(R1 + 6144, 512).rearrange("p (g q) -> p g q", g=4)
        bsb = at(R1 + 6656, 512).rearrange("p (g q) -> p g q", g=4)
        merged = at(R1 + 7168, DK * T).rearrange("p (k t) -> p k t", k=DK)
        B1 = R1 + R1_LEN
        aT = at(B1, 3072).rearrange("p (c t) -> p c t", c=4)
        mT = at(B1 + 3072, 3072).rearrange("p (c t) -> p c t", c=4)
        S0 = B1 + 6144
        sqn = at(S0, 4096)
        rn = at(S0 + 4096, 512)
        bias = at(S0, 3072).rearrange("p (b y k) -> p b y k", b=2, y=3)
        pr = at(S0 + 3072, 2304).rearrange("p (r k) -> p r k", r=3)
        ptr = at(S0 + 5376, 1536).rearrange("p (r k) -> p r k", r=2)
        sq = at(S0 + 6912, 2048).rearrange("p (r a k) -> p r a k", r=2, a=2)
        rr = at(S0 + 8960, 1024).rearrange("p (r k) -> p r k", r=2)
        sig = at(S0, 1536).rearrange("p (r k) -> p r k", r=3)
        prod = at(S0 + 1536, 1024).rearrange("p (r k) -> p r k", r=2)
        sgtmp = at(S0 + 2560, 1024).rearrange("p (r k) -> p r k", r=2)
        ub = at(0, U_RING * D).rearrange("p (r d) -> p r d", r=U_RING)
        vb = at(U_RING * D, V_RING * D).rearrange("p (r d) -> p r d", r=V_RING)
        qr = at(8192, 2 * T).rearrange("p (r t) -> p r t", r=2)
        kT = at(8192 + 2 * T, 256).rearrange("p (r t) -> p r t", r=2)
        o = 12288
        h2tok = at(o, 6 * D).rearrange("p (t d) -> p t d", t=6)
        o += 6 * D
        scores = at(o, 48 * 256)
        o += 48 * 256
        h2cur = at(o, D)
        tokout = at(o + D, D).rearrange("p (k q) -> p k q", k=DK)
        o += 2 * D
        dg = at(o, 256).rearrange("p (r q) -> p r q", r=2)
        sc = at(o + 256, 256).rearrange("p (a k) -> p a k", a=2)
        wk = at(o + 512, P)
        topv = at(o + 640, 32).rearrange("p (a k) -> p a k", a=2)
        topif = at(o + 672, 32).rearrange("p (a k) -> p a k", a=2)
        cand = at(o + 704, 256)
        cwk = at(o + 960, 256)
        oh = at(o + 1216, 256).rearrange("p (k j) -> p k j", k=16)
        best = at(o + 1472, 16)
        digit = at(o + 1488, 32).rearrange("p (a k) -> p a k", a=2)
        expert = at(o + 1520, 32).rearrange("p (a k) -> p a k", a=2)
        nbest = at(o + 1552, 1)
        gsum = at(o + 1553, IDX_RING)
        g2cur = at(o + 1560, DK)
        grcp = at(o + 1568, 1)
        zrow = at(o + 1570, P)
        topi = at(o + 1700, 32).bitcast(U32).rearrange("p (a k) -> p a k", a=2)
        pos = at(o + 1732, 16).bitcast(U32)
        dig = at(o + 1748, 32).bitcast(U32).rearrange("p (a k) -> p a k", a=2)

        banks = stack.enter_context(nc.psum_tensor("banks", [P, 8, 512], F))

        bank_full = [sem(f"bank_full{b}") for b in range(8)]
        bank_free = [sem(f"bank_free{b}") for b in range(8)]
        w_full = [sem(f"w_full{s}") for s in range(W_SLOTS)]
        const_in = sem("const_in")
        x_in = sem("x_in")
        c_in = sem("c_in")
        c_done = sem("c_done")
        small_in = sem("small_in")
        mod_done = sem("mod_done")
        sq_ready = sem("sq_ready")
        rt_ready = sem("rt_ready")
        xn_ready = sem("xn_ready")
        h_ready = sem("h_ready")
        nsq_ready = sem("nsq_ready")
        nrt_ready = sem("nrt_ready")
        item_done = sem("item_done")
        v_copied = sem("v_copied")
        vblk_in = sem("vblk_in")
        bias_in = sem("bias_in")
        bias_ready = sem("bias_ready")
        bias_zero = sem("bias_zero")
        eps_ready = sem("eps_ready")
        rope_done = sem("rope_done")
        bsb_in = sem("bsb_in")
        rows_made = sem("rows_made")
        pad_in = sem("pad_in")
        s_biased = sem("s_biased")
        neg_max = sem("neg_max")
        exp_done = sem("exp_done")
        p_ready = sem("p_ready")
        pt_ready = sem("pt_ready")
        pt_ready2 = sem("pt_ready2")
        kr_copied = sem("kr_copied")
        stage_end = sem("stage_end")
        sg_sq = sem("sg_sq")
        sg_rt = sem("sg_rt")
        sg_v = sem("sg_v")
        ws_ready = sem("ws_ready")
        sig_ready = sem("sig_ready")
        merged_ready = sem("merged_ready")
        x_ready = sem("x_ready")
        q_copied = sem("q_copied")
        kt_copied = sem("kt_copied")
        dve_chain = sem("dve_chain")
        act_chain = sem("act_chain")
        u_full = [sem(f"u_full{s}") for s in range(U_RING)]
        v_full = [sem(f"v_full{s}") for s in range(V_RING)]
        u_used = sem("u_used")
        v_used = sem("v_used")
        idx_ready = sem("idx_ready")
        best_ready = sem("best_ready")
        exp_gate = sem("exp_gate")
        gel_ready = sem("gel_ready")
        wgt_ready = sem("wgt_ready")
        diag_ready = sem("diag_ready")
        acc_start = sem("acc_start")
        acc_done = sem("acc_done")
        acc_copied = sem("acc_copied")
        outT_done = sem("outT_done")
        outT_added = sem("outT_added")
        pool_go = sem("pool_go")
        dve_go = sem("dve_go")
        zero_done = sem("zero_done")
        out_in = sem("out_in")

        jobs = {}
        last_use = {}
        loads = []
        load_at = {}

        def bank(b):
            return banks[:, b, :]

        SEG_CTX, SEG_LAT = (0, CTX), (CTX, SEQ)

        def segs(l, keys=False):
            return [SEG_CTX, SEG_LAT] if (l == 0 or keys) else [SEG_LAT]

        def tiles(l, keys=False):
            return list(range(6)) if (l == 0 or keys) else list(range(2, 6))

        def w_cols(w, l, c0, n):
            return w[l, :, c0:c0 + n].rearrange("(k p) n -> p k n", p=P)

        def add_load(name, parts):
            load_at[name] = len(loads)
            loads.append((name, parts))

        def plan_loads(l):
            for n in range(24):
                add_load((l, "mod", n), [(0, w_cols(w_mod, l, 256 * n, 256))])
            for what, c0 in (("q", C_Q), ("k", C_K), ("v", C_V)):
                for half in range(2):
                    add_load((l, what, half), [(0, w_cols(w_in, l, c0 + 256 * half, 256))])
            add_load((l, "cq", 0), [(0, w_cols(w_in, l, C_CQ, 256))])
            add_load((l, "ckv", 0), [(0, w_cols(w_in, l, C_CKV, KV_RANK + ROPE))])
            add_load((l, "uk", 0), [(0, mla_w_uk[l]), (512, mla_w_uv[l])])
            add_load((l, "uq", 0), [(0, w_cols(mla_w_uq, l, 0, HEADS * QK))])
            for what, c0 in (("u", C_U), ("sv", C_SV)):
                for half in range(2):
                    add_load((l, what, half), [(0, w_cols(w_in, l, c0 + 256 * half, 256))])
            add_load((l, "sgw", 0), [(0, sg_w[l].rearrange("g p q -> p g q"))])
            for b in range(3):
                for half in range(2):
                    add_load((l, "wb", b, half), [(0, w_branch[l, b, :, 512 * half:512 * half + 512]
                                                   .rearrange("(k p) n -> p k n", p=P))])
                    for q in range(2):
                        add_load((l, "gt", b, half, q),
                                 [(0, w_cols(w_in, l, C_GATE + D * b + 512 * half + 256 * q, 256))])
            for q in range(4):
                add_load((l, "wo", q), [(0, w_cols(w_out, l, 256 * q, 256))])
            add_load((l, "pk", 0), [(0, peer_k1[l]), (128, peer_k2[l])])
            for q in range(8):
                add_load((l, "pq", q), [(0, w_cols(peer_w_q, l, 256 * q, 256))])

        for l in range(LAYERS):
            plan_loads(l)

        def w_value(name):
            n = load_at[name]
            return n % W_SLOTS, 16 * sum(len(loads[m][1]) for m in range(n % W_SLOTS, n + 1, W_SLOTS))

        def na_items(l):
            out_ = []
            for what, dest, g, keys in (("q", naq, G_Q, False), ("k", nak, G_K, True)):
                for ch in range(4):
                    for s0, n in segs(l, keys):
                        out_.append(dict(key=(l, what, ch, s0), load=(l, what, ch // 2), s0=s0, n=n, p0=0, p1=P,
                                         raw=[[("h", k, k * 256 + (ch % 2) * P, P) for k in range(DK)]],
                                         norm=blk64, scale=1.0, gain=[g], dest=[dest[:, ch, s0:s0 + n]], rope=None))
            return out_

        def latent_items(l):
            out_ = []
            for s0, n in segs(l):
                out_.append(dict(key=(l, "cq", s0), load=(l, "cq", 0), s0=s0, n=n, p0=0, p1=P,
                                 raw=[[("h", k, k * 256 + a * P, P) for k in range(DK)] for a in range(2)],
                                 norm=ones, scale=4.0, gain=[G_CQ, G_CQ + 1],
                                 dest=[cqT[:, a, s0:s0 + n] for a in range(2)], rope=None))
            for s0, n in segs(l, True):
                out_.append(dict(key=(l, "ckv", s0), load=(l, "ckv", 0), s0=s0, n=n, p0=0, p1=P,
                                 raw=[[("h", k, k * 160, P) for k in range(DK)]],
                                 norm=ones, scale=8.0, gain=[G_CKV], dest=[ckvT[:, s0:s0 + n]], rope=None))
            for s0, n in segs(l, True):
                out_.append(dict(key=(l, "kr", s0), load=(l, "ckv", 0), s0=s0, n=n, p0=64, p1=96,
                                 raw=[[("h", k, k * 160 + P, ROPE) for k in range(DK)]],
                                 norm=blkq, scale=1.0, gain=[G_KR], dest=[krT[64:96, s0:s0 + n]],
                                 rope=krT[64:96, s0:s0 + n] if s0 else None))
            return out_

        def head_items(l, grp):
            out_ = []
            for hh in range(4):
                h = 4 * grp + hh
                for s0, n in segs(l):
                    out_.append(dict(key=(l, "mq", h, s0), load=(l, "uq", 0), s0=s0, n=n, p0=0, p1=QK,
                                     raw=[[("cq", k, k * 768 + h * QK, QK) for k in range(2)]],
                                     norm=blkq, scale=1.0, gain=[G_QQ], dest=[qm[0:QK, hh, s0:s0 + n]],
                                     rope=qm[64:96, hh, s0:s0 + n] if s0 else None))
                for s0, n in segs(l, True):
                    out_.append(dict(key=(l, "mk", h, s0), load=(l, "uk", 0), s0=s0, n=n, p0=0, p1=64,
                                     raw=[[("ckv", 0, h * 64, 64)]],
                                     norm=blk64, scale=1.0, gain=[G_KN], dest=[km[0:64, hh, s0:s0 + n]], rope=None))
            return out_

        def na_units(l):
            out_ = []
            for h in range(HEADS):
                p0 = 64 * (h % 2)
                qh, kh = naq[p0:p0 + 64, h // 2, :], nak[p0:p0 + 64, h // 2, :]
                fcols = slice(64 * h, 64 * h + 64)
                ah = aT[p0:p0 + 64, h // 2, :]
                for n in range(NBLK):
                    start = min(max(n * COL_BLK - WIN_C // 2, 0), GRID_W - KEY_COLS)
                    grid_k = kh[:, CTX:T].rearrange("p (r w) -> p r w", w=GRID_W)[:, :, start:start + KEY_COLS]
                    grid_a = ah[:, CTX:T].rearrange("p (r w) -> p r w", w=GRID_W)[:, :, n * COL_BLK:(n + 1) * COL_BLK]
                    out_.append(dict(key=(l, "na", h, n), pieces=[512], q=qh[:, CTX + n * P:CTX + (n + 1) * P],
                                     k=[(0, 0, NLOC, grid_k), (0, NLOC, 512, kh[:, 0:CTX])],
                                     bias=(h, KIND[n]), scale=0.125, po=p0,
                                     v=[vblk[:, n, 0, fcols], vblk[:, n, 1, fcols], vna[:, 0, fcols], vna[:, 1, fcols]],
                                     dest=grid_a))
            if l == 0:
                for h in range(HEADS):
                    p0 = 64 * (h % 2)
                    for t in range(2):
                        out_.append(dict(key=(l, "nac", h, t), pieces=[CTX],
                                         q=naq[p0:p0 + 64, h // 2, t * P:(t + 1) * P],
                                         k=[(0, 0, CTX, nak[p0:p0 + 64, h // 2, 0:CTX])], bias=None, scale=0.125, po=p0,
                                         v=[vna[:, a, 64 * h:64 * h + 64] for a in range(2)],
                                         dest=aT[p0:p0 + 64, h // 2, t * P:(t + 1) * P]))
            return out_

        def mla_units(l, grp):
            out_ = []
            for hh in range(4):
                h = 4 * grp + hh
                p0 = 64 * (h % 2)
                for t in tiles(l):
                    nk = T if t >= 2 else CTX
                    pieces = [512, 256] if nk == T else [256]
                    ks = [(a, 0, w, km[0:QK, hh, 512 * a:512 * a + w]) for a, w in enumerate(pieces)]
                    out_.append(dict(key=(l, "mla", h, t), pieces=pieces, q=qm[0:QK, hh, t * P:(t + 1) * P], k=ks,
                                     bias=None, scale=float(QK) ** -0.5, po=p0,
                                     v=[vm[:, a, 64 * h:64 * h + 64] for a in range(nk // P)],
                                     dest=mT[p0:p0 + 64, h // 2, t * P:(t + 1) * P]))
            return out_

        block = stack.enter_context(nc.Block())

        def barrier(eng, n):
            eng.drain().then_inc(stage_end, 1)
            eng.wait_ge(stage_end, 4 * n)

        def stage_no(l, k):
            return 7 * l + k

        def PEER_TILES(l):
            return (0, 6) if l == 0 else (2, 6)

        @block.tensor
        def _(pe):
            cnt = dict(sq=0, nsq=0, item=0, p=0, pt=0, pt2=0, rope=0)

            def fill(key):
                j = len(jobs)
                b, use = j % 8, j // 8
                jobs[key] = (b, use)
                if use:
                    pe.wait_ge(bank_free[b], use)
                return bank(b)

            def filled(ins, key):
                ins.then_inc(bank_full[jobs[key][0]], 1)

            def weights(name, key):
                s, v = w_value(name)
                pe.wait_ge(w_full[s], v)
                last_use[name] = key
                return wring[:, s, :]

            def norm_sum(l, which, i, s0, n):
                key = (l, which, s0)
                bk = fill(key)
                cnt["nsq"] += 1
                pe.wait_ge(nsq_ready, cnt["nsq"])
                for k in range(DK):
                    ins = nc.tensor.matmul(bk[:, 0:n], ones, sqn[:, k * n:(k + 1) * n], start=(k == 0), stop=(k == DK - 1))
                filled(ins, key)

            def moving(kind, k, s0, n):
                if kind == "h":
                    return hT[:, k, s0:s0 + n]
                return cqT[:, k, s0:s0 + n] if kind == "cq" else ckvT[:, s0:s0 + n]

            def run_items(items):
                base = cnt["item"]
                for i in range(len(items) + 2):
                    if i < len(items):
                        it = items[i]
                        for a, terms in enumerate(it["raw"]):
                            key = it["key"] + ("raw", a)
                            bk = fill(key)
                            w = weights(it["load"], key)
                            for m, (kind, k, wo, wn) in enumerate(terms):
                                ins = nc.tensor.matmul(bk[it["p0"]:it["p1"], 0:it["n"]], w[:, wo:wo + wn],
                                                       moving(kind, k, it["s0"], it["n"]),
                                                       start=(m == 0), stop=(m == len(terms) - 1))
                            filled(ins, key)
                    if 1 <= i <= len(items):
                        it = items[i - 1]
                        key = it["key"] + ("norm",)
                        bk = fill(key)
                        cnt["sq"] += 1
                        pe.wait_ge(sq_ready, cnt["sq"])
                        p0, p1 = it["p0"], it["p1"]
                        na = len(it["raw"])
                        for a in range(na):
                            ins = nc.tensor.matmul(bk[p0:p1, 0:it["n"]], it["norm"][p0:p1, p0:p1],
                                                   sq[p0:p1, (i - 1) % 2, a, 0:it["n"]], start=(a == 0), stop=(a == na - 1))
                        filled(ins, key)
                    if i >= 2 and items[i - 2]["rope"] is not None:
                        it = items[i - 2]
                        key = it["key"] + ("rope",)
                        bk = fill(key)
                        pe.wait_ge(item_done, base + i - 1)
                        ins = nc.tensor.matmul(bk[64:96, 0:it["n"]], rot[64:96, 64:96], it["rope"], start=True, stop=True)
                        filled(ins, key)
                cnt["item"] = base + len(items)
                pe.wait_ge(item_done, cnt["item"])
                cnt["rope"] += sum(it["rope"] is not None for it in items)
                if cnt["rope"]:
                    pe.wait_ge(rope_done, cnt["rope"])

            def run_units(units):
                for i in range(len(units) + 3):
                    if i < len(units):
                        un = units[i]
                        for a, w in enumerate(un["pieces"]):
                            key = un["key"] + ("s", a)
                            bk = fill(key)
                            for pa, c0, c1, kk in un["k"]:
                                if pa == a:
                                    ins = nc.tensor.matmul(bk[:, c0:c1], un["q"], kk, start=True, stop=True)
                            filled(ins, key)
                    if 2 <= i < len(units) + 2:
                        un = units[i - 2]
                        cnt["p"] += 1
                        pe.wait_ge(p_ready, cnt["p"])
                        for a, w in enumerate(un["pieces"]):
                            key = un["key"] + ("t", a)
                            bk = fill(key)
                            for j in range(w // P):
                                ins = nc.tensor.transpose(bk[:, j * P:(j + 1) * P],
                                                          pr[:, (i - 2) % 3, 512 * a + j * P:512 * a + (j + 1) * P], ident)
                            filled(ins, key)
                    if 3 <= i:
                        un = units[i - 3]
                        key = un["key"] + ("o",)
                        bk = fill(key)
                        cnt["pt"] += 1
                        pe.wait_ge(pt_ready, cnt["pt"])
                        if len(un["pieces"]) > 1:
                            cnt["pt2"] += 1
                            pe.wait_ge(pt_ready2, cnt["pt2"])
                        nv = len(un["v"])
                        for j, vv in enumerate(un["v"]):
                            ins = nc.tensor.matmul(bk[un["po"]:un["po"] + 64, 0:P], vv, ptr[:, (i - 3) % 2, j * P:(j + 1) * P],
                                                   start=(j == 0), stop=(j == nv - 1))
                        filled(ins, key)

            def feature_job(key, load, wo, s0, n, terms=DK, step=256, src=None):
                bk = fill(key)
                w = weights(load, key)
                src = hT if src is None else src
                for k in range(terms):
                    ins = nc.tensor.matmul(bk[:, 0:n], w[:, k * step + wo:k * step + wo + P], src[:, k, s0:s0 + n],
                                           start=(k == 0), stop=(k == terms - 1))
                filled(ins, key)

            pe.wait_ge(const_in, 16)
            hcount = 0
            for l in range(LAYERS):
                pe.wait_ge(c_done, 1)
                for n in range(24):
                    key = (l, "mod", n)
                    bk = fill(key)
                    w = weights(key, key)
                    for a in range(2):
                        for k in range(DK):
                            ins = nc.tensor.matmul(bk[:, 2 * a:2 * a + 2], w[:, k * 256 + a * P:k * 256 + a * P + P],
                                                   cS[:, k, :], start=(k == 0), stop=(k == DK - 1))
                    filled(ins, key)
                for i, (s0, n) in enumerate(segs(l, True)):
                    norm_sum(l, "n1", i, s0, n)
                hcount += 2
                pe.wait_ge(h_ready, hcount)
                run_items(na_items(l))
                for half in range(2):
                    for t in tiles(l, True):
                        key = (l, "v", half, t)
                        bk = fill(key)
                        w = weights((l, "v", half), key)
                        for k in range(DK):
                            ins = nc.tensor.matmul(bk[:, 0:256], hT[:, k, t * P:(t + 1) * P], w[:, k * 256:(k + 1) * 256],
                                                   start=(k == 0), stop=(k == DK - 1))
                        filled(ins, key)
                pe.wait_ge(vblk_in, 16 * 32 * (l + 1))
                run_units(na_units(l))
                barrier(pe, stage_no(l, 1))
                run_items(latent_items(l))
                for t in tiles(l, True):
                    key = (l, "vm", t)
                    bk = fill(key)
                    w = weights((l, "uk", 0), key)
                    filled(nc.tensor.matmul(bk, ckvT[:, t * P:(t + 1) * P], w[:, 512:1024], start=True, stop=True), key)
                for grp in range(2):
                    run_items(head_items(l, grp))
                    pe.wait_ge(kr_copied, 4 * (l + 1))
                    run_units(mla_units(l, grp))
                    barrier(pe, stage_no(l, 2 + grp))
                for ch in range(4):
                    for s0, n in segs(l):
                        feature_job((l, "u", ch, s0), (l, "u", ch // 2), (ch % 2) * P, s0, n)
                for half in range(2):
                    for t in tiles(l):
                        key = (l, "sv", half, t)
                        bk = fill(key)
                        w = weights((l, "sv", half), key)
                        for k in range(DK):
                            ins = nc.tensor.matmul(bk[:, 0:256], hT[:, k, t * P:(t + 1) * P], w[:, k * 256:(k + 1) * 256],
                                                   start=(k == 0), stop=(k == DK - 1))
                        filled(ins, key)
                key = (l, "wsT")
                bk = fill(key)
                w = weights((l, "sgw", 0), key)
                for g in range(GROUPS):
                    ins = nc.tensor.transpose(bk[:, g * P:(g + 1) * P], w[:, g * P:(g + 1) * P], ident)
                filled(ins, key)
                pe.wait_ge(ws_ready, l + 1)
                for i, t in enumerate(tiles(l)):
                    key = (l, "mix", t)
                    bk = fill(key)
                    pe.wait_ge(sg_v, (0 if l == 0 else 6) + i + 1)
                    for g in range(GROUPS):
                        ins = nc.tensor.matmul(bk[:, g * P:(g + 1) * P], vg[:, t, g * P:(g + 1) * P], wsT[:, g, :],
                                               start=True, stop=True)
                    filled(ins, key)
                barrier(pe, stage_no(l, 4))
                src = [aT, uT, mT]
                for b in range(3):
                    for ch in range(8):
                        half, q = ch // 4, (ch % 4) // 2
                        for s0, n in segs(l):
                            feature_job((l, "g", b, ch, s0), (l, "gt", b, half, q), (ch % 2) * P, s0, n)
                            feature_job((l, "b", b, ch, s0), (l, "wb", b, half), (ch % 4) * P, s0, n, 4, 512, src[b])
                pe.wait_ge(merged_ready, l + 1)
                for ch in range(8):
                    for s0, n in segs(l):
                        feature_job((l, "o", ch, s0), (l, "wo", ch // 2), (ch % 2) * P, s0, n, src=merged)
                for i, (s0, n) in enumerate(segs(l)):
                    norm_sum(l, "n2", i, s0, n)
                hcount += len(segs(l))
                pe.wait_ge(h_ready, hcount)
                barrier(pe, stage_no(l, 5))
                key = (l, "kT")
                bk = fill(key)
                w = weights((l, "pk", 0), key)
                for a in range(2):
                    ins = nc.tensor.transpose(bk[:, a * P:(a + 1) * P], w[:, a * P:(a + 1) * P], ident)
                filled(ins, key)
                pe.wait_ge(kt_copied, l + 1)
                for t in tiles(l):
                    for half in range(2):
                        key = (l, "h2", t, half)
                        bk = fill(key)
                        for j in range(4):
                            ins = nc.tensor.transpose(bk[:, j * P:(j + 1) * P], hT[:, 4 * half + j, t * P:(t + 1) * P], ident)
                        filled(ins, key)
                ns = len(segs(l))
                for ch in range(17):
                    if ch < 16:
                        for s0, n in segs(l):
                            feature_job((l, "pq", ch, s0), (l, "pq", ch // 2), (ch % 2) * P, s0, n)
                    if ch >= 1:
                        cc = ch - 1
                        pe.wait_ge(q_copied, (32 * l) + ns * (cc + 1))
                        for g, tt in enumerate((tiles(l)[:4], tiles(l)[4:])):
                            if tt:
                                key = (l, "sc", cc, g)
                                bk = fill(key)
                                for j, t in enumerate(tt):
                                    ins = nc.tensor.matmul(bk[:, j * P:(j + 1) * P], qr[:, cc % 2, t * P:(t + 1) * P],
                                                           kT[:, cc % 2, :], start=True, stop=True)
                                filled(ins, key)
                nj = len(jobs)
                for b in range(8):
                    pe.wait_ge(bank_free[b], (nj - b + 7) // 8)
                barrier(pe, stage_no(l, 6))
                t0, t1 = PEER_TILES(l)
                done_tiles = 0 if l == 0 else 6
                pe.wait_ge(zero_done, l + 1)
                with pe.Fori(0, t1 - t0) as t:
                    tile = t + done_tiles
                    for a in range(2):
                        nc.tensor.matmul(bank(a), zrow, consts[:, 0:512], start=True, stop=False, skip_group_check=True)
                    for j in range(128):
                        pe.wait_ge(diag_ready, tile * 128 + (j + 1))
                        pe.wait_ge(v_full[j % V_RING], tile * (16 * 128 // V_RING) + 16 * (j // V_RING + 1))
                        for a in range(2):
                            ins = nc.tensor.matmul(bank(a), dg[:, j % 2, :], vb[:, j % V_RING, a * 512:(a + 1) * 512],
                                                   start=False, stop=(j == 127), skip_group_check=True)
                        ins.then_inc(v_used, 1)
                    pe.wait_ge(acc_copied, tile * 2 + 2)
                    for k in range(DK):
                        ins = nc.tensor.transpose(banks[:, 2 + k // 4, (k % 4) * P:(k % 4 + 1) * P], tokout[:, k, :], ident)
                    ins.then_inc(outT_done, 1)
                    pe.wait_ge(outT_added, tile * DK + DK)
                barrier(pe, stage_no(l, 7))

        def reader(eng, key):
            b, use = jobs[key]
            eng.wait_ge(bank_full[b], use + 1)
            return bank(b)

        def freed(eng, ins, key, wait=False):
            b, use = jobs[key]
            ins.then_inc(bank_free[b], 1)
            if wait:
                eng.wait_ge(bank_free[b], use + 1)

        @block.scalar
        def _(act):
            chain = [0]
            cnt = dict(sqn=0, nrt=0, xn=0, sq=0, item=0, neg=0, sb_=0, exp=0, u=0, sgv=0)

            def link(ins):
                chain[0] += 1
                ins.then_inc(act_chain, 1)
                act.wait_ge(act_chain, chain[0])

            def norm(l, which, sg_list):
                for s0, n in sg_list:
                    if x_val[0]:
                        act.wait_ge(x_ready, x_val[0])
                    if last_norm[0] is not None:
                        b, use = jobs[last_norm[0]]
                        act.wait_ge(bank_full[b], use + 1)
                    nc.scalar.activation(sqn[:, 0:DK * n].rearrange("p (k t) -> p k t", k=DK), X[:, :, s0:s0 + n],
                                         ACT.Square).then_inc(nsq_ready, 1)
                    key = (l, which, s0)
                    last_norm[0] = key
                    bk = reader(act, key)
                    if cnt["nrt"]:
                        act.wait_ge(xn_ready, cnt["xn"])
                    freed(act, nc.scalar.activation(rn[:, 0:n], bk[:, 0:n], ACT.Sqrt, bias=epsc[:, 0:1]), key, True)
                    act.sem_inc(nrt_ready, 1)
                    cnt["nrt"] += 1
                    gs, sh = (gs1, 0) if which == "n1" else (gs2, 3)
                    act.wait_ge(mod_done, l + 1)
                    strm = 1 if s0 == 0 else 0
                    for k in range(DK):
                        cnt["xn"] += 1
                        act.wait_ge(xn_ready, cnt["xn"])
                        ins = nc.scalar.activation(hT[:, k, s0:s0 + n], hT[:, k, s0:s0 + n], ACT.Identity,
                                                   scale=gs[:, strm, k:k + 1], bias=modc[:, 8 * sh + k, strm:strm + 1])
                    ins.then_inc(h_ready, 1)

            def run_items(items):
                for i in range(len(items) + 1):
                    if i < len(items):
                        it = items[i]
                        p0, p1 = it["p0"], it["p1"]
                        if i >= 2:
                            b, use = jobs[items[i - 2]["key"] + ("norm",)]
                            act.wait_ge(bank_full[b], use + 1)
                        for a in range(len(it["raw"])):
                            bk = reader(act, it["key"] + ("raw", a))
                            ins = nc.scalar.activation(sq[p0:p1, i % 2, a, 0:it["n"]], bk[p0:p1, 0:it["n"]], ACT.Square)
                        ins.then_inc(sq_ready, 1)
                    if i >= 1:
                        it = items[i - 1]
                        p0, p1 = it["p0"], it["p1"]
                        key = it["key"] + ("norm",)
                        bk = reader(act, key)
                        if i >= 3:
                            act.wait_ge(item_done, cnt["item"] + i - 2)
                        freed(act, nc.scalar.activation(rr[p0:p1, (i - 1) % 2, 0:it["n"]], bk[p0:p1, 0:it["n"]],
                                                        ACT.Sqrt, scale=it["scale"], bias=epsc[p0:p1, 0:1]), key)
                cnt["item"] += len(items)

            def run_units(units):
                u0 = cnt["u"]
                for i in range(len(units) + 3):
                    if i < len(units):
                        un = units[i]
                        cnt["neg"] += 1
                        act.wait_ge(neg_max, cnt["neg"])
                        st = stats[:, i % 4, :]
                        if i >= 3 and un["bias"] is None:
                            b, use = jobs[units[i - 3]["key"] + ("t", len(units[i - 3]["pieces"]) - 1)]
                            act.wait_ge(bank_full[b], use + 1)
                        for a, w in enumerate(un["pieces"]):
                            dst = pr[:, i % 3, 512 * a:512 * a + w]
                            if un["bias"] is not None:
                                ins = nc.scalar.activation(dst, dst, ACT.Exp, bias=st[:, 2:3], accum_out=st[:, 4 + a:5 + a])
                                ins.then_inc(exp_done, 1)
                                cnt["exp"] += 1
                            else:
                                key = un["key"] + ("s", a)
                                bk = reader(act, key)
                                freed(act, nc.scalar.activation(dst, bk[:, 0:w], ACT.Exp, bias=st[:, 2:3], scale=un["scale"],
                                                                accum_out=st[:, 4 + a:5 + a]), key)
                    if 2 <= i < len(units) + 2:
                        un = units[i - 2]
                        if i >= 4:
                            b, use = jobs[units[i - 4]["key"] + ("o",)]
                            act.wait_ge(bank_full[b], use + 1)
                        key = un["key"] + ("t", 0)
                        bk = reader(act, key)
                        w = un["pieces"][0]
                        freed(act, nc.scalar.activation(ptr[:, (i - 2) % 2, 0:w], bk[:, 0:w], ACT.Copy), key, True)
                        act.sem_inc(pt_ready, 1)
                    if 3 <= i:
                        un = units[i - 3]
                        key = un["key"] + ("o",)
                        bk = reader(act, key)
                        po = un["po"]
                        src = bk[po:po + 64, 0:P]
                        if len(un["dest"].shape) == 3:
                            src = src.rearrange("p (r w) -> p r w", w=COL_BLK)
                        freed(act, nc.scalar.activation(un["dest"], src, ACT.Copy), key)
                cnt["u"] += len(units)

            last_norm = [None]
            x_val = [0]
            act.wait_ge(c_in, 16)
            link(nc.scalar.activation(cS[:, :, :], cT[:, :, :], ACT.Sigmoid))
            act.wait_ge(x_in, 16 * 12)
            act.wait_ge(eps_ready, 1)
            for l in range(LAYERS):
                norm(l, "n1", segs(l, True))
                run_items(na_items(l))
                for half in range(2):
                    for t in tiles(l, True):
                        key = (l, "v", half, t)
                        bk = reader(act, key)
                        freed(act, nc.scalar.activation(vna[:, t, half * 256:(half + 1) * 256], bk[:, 0:256], ACT.Copy), key, True)
                act.sem_inc(v_copied, 1)
                run_units(na_units(l))
                barrier(act, stage_no(l, 1))
                run_items(latent_items(l))
                for t in tiles(l, True):
                    key = (l, "vm", t)
                    bk = reader(act, key)
                    freed(act, nc.scalar.activation(vm[:, t, :], bk, ACT.Copy), key)
                for grp in range(2):
                    run_items(head_items(l, grp))
                    run_units(mla_units(l, grp))
                    barrier(act, stage_no(l, 2 + grp))
                for ch in range(4):
                    for s0, n in segs(l):
                        key = (l, "u", ch, s0)
                        bk = reader(act, key)
                        freed(act, nc.scalar.activation(uT[:, ch, s0:s0 + n], bk[:, 0:n], ACT.Gelu_apprx_tanh), key)
                for half in range(2):
                    for t in tiles(l):
                        key = (l, "sv", half, t)
                        bk = reader(act, key)
                        freed(act, nc.scalar.activation(vg[:, t, half * 256:(half + 1) * 256], bk[:, 0:256],
                                                        ACT.Gelu_apprx_tanh), key, True)
                key = (l, "wsT")
                bk = reader(act, key)
                freed(act, nc.scalar.activation(wsT, bk.rearrange("p (g q) -> p g q", g=4), ACT.Copy), key, True)
                act.sem_inc(ws_ready, 1)
                for i, t in enumerate(tiles(l)):
                    link(nc.scalar.activation(sgtmp[:, 0, :], vg[:, t, :], ACT.Square, accum_out=stats[:, i % 4, 6:7]))
                    cnt["sgv"] += 1
                    if i >= 4:
                        act.wait_ge(sg_v, cnt["sgv"] - 4)
                    link(nc.scalar.activation(stats[:, i % 4, 7:8], stats[:, i % 4, 6:7], ACT.Sqrt, scale=1.0 / SG_W,
                                              bias=epsc[:, 0:1]))
                    act.sem_inc(sg_rt, 1)
                barrier(act, stage_no(l, 4))
                n_sig, sig_hist = 0, []
                for b in range(3):
                    for ch in range(8):
                        for s0, n in segs(l):
                            key = (l, "g", b, ch, s0)
                            bk = reader(act, key)
                            if n_sig >= 3:
                                kb, ku = jobs[sig_hist[n_sig - 3]]
                                act.wait_ge(bank_free[kb], ku + 1)
                            sig_hist.append((l, "b", b, ch, s0))
                            freed(act, nc.scalar.activation(sig[:, n_sig % 3, 0:n], bk[:, 0:n], ACT.Sigmoid), key, True)
                            act.sem_inc(sig_ready, 1)
                            n_sig += 1
                x_val[0] = 2 * l + 1
                norm(l, "n2", segs(l))
                barrier(act, stage_no(l, 5))
                for ch in range(16):
                    for s0, n in segs(l):
                        key = (l, "pq", ch, s0)
                        bk = reader(act, key)
                        if ch >= 2:
                            g = 1 if l == 0 else 0
                            b, use = jobs[(l, "sc", ch - 2, g)]
                            act.wait_ge(bank_full[b], use + 1)
                        freed(act, nc.scalar.activation(qr[:, ch % 2, s0:s0 + n], bk[:, 0:n], ACT.Copy), key, True)
                        act.sem_inc(q_copied, 1)
                barrier(act, stage_no(l, 6))
                t0, t1 = PEER_TILES(l)
                nt = t1 - t0
                unit0 = 0 if l == 0 else 48
                tile0 = 0 if l == 0 else 6

                def exp_best(e):
                    ev, slot = e
                    act.wait_ge(best_ready, ev)
                    nc.scalar.activation(gate[:, slot, :], best, ACT.Exp, bias=nbest,
                                         accum_out=gsum[:, slot:slot + 1]).then_inc(exp_gate, 1)

                def gelu_dots(ev16, ev, r):
                    act.wait_ge(u_used, ev16)
                    act.activation(gel[:, r, :], dots[:, r, :], ACT.Gelu_apprx_tanh).then_inc(gel_ready, 1)

                exp_best((unit0 + 1, 0))
                exp_best((unit0 + 2, 1))
                gelu_dots(unit0 * 16 + 16, 0, 0)

                def peer_tile(t, last, first):
                    for j in range(8):
                        tu = t * 8 + unit0
                        for k in range(16):
                            if k == 0:
                                act.wait_ge(wgt_ready, tu + (j + 1))
                            if not (first and not unit0 and j == 0 and k < 2):
                                act.wait_ge(v_used, t * 128 + (unit0 * 16 + 16 * j + k - 1))
                            act.activation(dg[:, k % 2, :], ident, ACT.Copy, scale=wgt[:, j % 2, k:k + 1]).then_inc(diag_ready, 1)
                            if k == 13 and not (last and j >= 6):
                                exp_best((tu + (j + 3), (j + 2) % 4))
                        if not (last and j == 7):
                            gelu_dots(t * 128 + (unit0 * 16 + 16 * (j + 2)), 0, (j + 1) % 2)
                    for a in range(2):
                        if a == 0:
                            act.wait_ge(v_used, t * 128 + (unit0 * 16 + 128))
                        act.activation(tokout[:, 4 * a:4 * a + 4, :], bank(a).rearrange("p (k q) -> p k q", k=4),
                                       ACT.Copy).then_inc(acc_copied, 1)

                peer_tile(0, nt == 1, True)
                if nt > 2:
                    with act.Fori(1, nt - 1) as t:
                        peer_tile(t, False, False)
                peer_tile(nt - 1, True, False)
                x_val[0] = 2 * l + 2
                barrier(act, stage_no(l, 7))

        @block.vector
        def _(dve):
            chain = [0]
            cnt = dict(nrt=0, item=0, bias=0, exp=0, sg=0, sig=0)

            def link(ins):
                chain[0] += 1
                ins.then_inc(dve_chain, 1)
                dve.wait_ge(dve_chain, chain[0])

            def norm(l, which, sg_list):
                for s0, n in sg_list:
                    cnt["nrt"] += 1
                    dve.wait_ge(nrt_ready, cnt["nrt"])
                    link(nc.vector.reciprocal(rn[:, 0:n], rn[:, 0:n]))
                    for k in range(DK):
                        nc.vector.tensor_tensor(hT[:, k, s0:s0 + n], X[:, k, s0:s0 + n], rn[:, 0:n],
                                                ALU.mult).then_inc(xn_ready, 1)

            def run_items(items):
                for i in range(len(items) + 1):
                    if i < len(items):
                        it = items[i]
                        p0, p1, n = it["p0"], it["p1"], it["n"]
                        b, use = jobs[it["key"] + ("norm",)]
                        dve.wait_ge(bank_free[b], use + 1)
                        link(nc.vector.reciprocal(rr[p0:p1, i % 2, 0:n], rr[p0:p1, i % 2, 0:n]))
                        for a, dst in enumerate(it["dest"]):
                            key = it["key"] + ("raw", a)
                            bk = reader(dve, key)
                            g = it["gain"][a]
                            if it["key"][1] == "q" and it["s0"]:
                                grid = bk[:, 0:SEQ].rearrange("p (r w) -> p r w", w=GRID_W)
                                root = rr[:, i % 2, :].rearrange("p (r w) -> p r w", w=GRID_W)
                                for m in range(NBLK):
                                    cols = slice(m * COL_BLK, (m + 1) * COL_BLK)
                                    ins = nc.vector.scalar_tensor_tensor(
                                        out=dst[:, m * P:(m + 1) * P].rearrange("p (r w) -> p r w", w=COL_BLK),
                                        in0=grid[:, :, cols], scalar=gains[:, g:g + 1], in1=root[:, :, cols],
                                        op0=ALU.mult, op1=ALU.mult)
                                freed(dve, ins, key, True)
                                continue
                            freed(dve, nc.vector.scalar_tensor_tensor(
                                out=dst, in0=bk[p0:p1, 0:n], scalar=gains[p0:p1, g:g + 1],
                                in1=rr[p0:p1, i % 2, 0:n], op0=ALU.mult, op1=ALU.mult), key, True)
                        dve.sem_inc(item_done, 1)
                    if i >= 1 and items[i - 1]["rope"] is not None:
                        it = items[i - 1]
                        r, n = it["rope"], it["n"]
                        key = it["key"] + ("rope",)
                        bk = reader(dve, key)
                        link(nc.vector.tensor_tensor(r, r, cosT[64:96, :], ALU.mult))
                        freed(dve, nc.vector.tensor_tensor(rtmp[64:96, 0:n], bk[64:96, 0:n], sinT[64:96, :], ALU.mult), key, True)
                        link(nc.vector.tensor_tensor(r, r, rtmp[64:96, 0:n], ALU.add))
                        dve.sem_inc(rope_done, 1)

            rtmp = at(S0, 512)

            def run_units(units):
                for i in range(len(units) + 2):
                    if i < len(units):
                        un = units[i]
                        st = stats[:, i % 4, :]
                        npc = len(un["pieces"])
                        if un["bias"] is not None:
                            h, kind = un["bias"]
                            if i >= 3:
                                b, use = jobs[units[i - 3]["key"] + ("t", len(units[i - 3]["pieces"]) - 1)]
                                dve.wait_ge(bank_full[b], use + 1)
                            key = un["key"] + ("s", 0)
                            bk = reader(dve, key)
                            dve.wait_ge(bias_ready, 8 * (un["key"][0]) + h + 1)
                            freed(dve, nc.vector.scalar_tensor_tensor(
                                out=pr[:, i % 3, 0:512], in0=bk, scalar=un["scale"], in1=bias[:, h % 2, kind, :],
                                op0=ALU.mult, op1=ALU.add), key, True)
                            nc.vector.tensor_reduce(st[:, 2:3], pr[:, i % 3, 0:512], axis=AX.X, op=ALU.max,
                                                    negate=True).then_inc(neg_max, 1)
                        else:
                            for a, w in enumerate(un["pieces"]):
                                bk = reader(dve, un["key"] + ("s", a))
                                ins = nc.vector.tensor_reduce(st[:, a:a + 1], bk[:, 0:w], axis=AX.X, op=ALU.max)
                                link(ins)
                            if npc == 2:
                                link(nc.vector.tensor_tensor(st[:, 0:1], st[:, 0:1], st[:, 1:2], ALU.max))
                            nc.vector.tensor_scalar(st[:, 2:3], st[:, 0:1], -un["scale"], None, ALU.mult).then_inc(neg_max, 1)
                    if 1 <= i <= len(units):
                        un = units[i - 1]
                        st = stats[:, (i - 1) % 4, :]
                        npc = len(un["pieces"])
                        if un["bias"] is not None:
                            cnt["exp"] += 1
                            dve.wait_ge(exp_done, cnt["exp"])
                        else:
                            for a in range(npc):
                                b, use = jobs[un["key"] + ("s", a)]
                                dve.wait_ge(bank_free[b], use + 1)
                        if npc == 2:
                            link(nc.vector.tensor_tensor(st[:, 4:5], st[:, 4:5], st[:, 5:6], ALU.add))
                        link(nc.vector.reciprocal(st[:, 3:4], st[:, 4:5]))
                        w = sum(un["pieces"])
                        nc.vector.tensor_scalar(pr[:, (i - 1) % 3, 0:w], pr[:, (i - 1) % 3, 0:w], st[:, 3:4], None,
                                                ALU.mult).then_inc(p_ready, 1)
                    if 2 <= i:
                        pt2(units, i - 2)

            def pt2(units, m):
                un = units[m]
                if len(un["pieces"]) < 2:
                    return
                if m >= 2:
                    b, use = jobs[units[m - 2]["key"] + ("o",)]
                    dve.wait_ge(bank_full[b], use + 1)
                key = un["key"] + ("t", 1)
                bk = reader(dve, key)
                w = un["pieces"][1]
                freed(dve, nc.vector.tensor_copy(ptr[:, m % 2, 512:512 + w], bk[:, 0:w]), key, True)
                dve.sem_inc(pt_ready2, 1)

            dve.wait_ge(c_in, 16)
            dve.wait_ge(act_chain, 1)
            nc.vector.tensor_tensor(cS[:, :, :], cS[:, :, :], cT[:, :, :], ALU.mult).then_inc(c_done, 1)
            for l in range(LAYERS):
                dve.wait_ge(small_in, 32 * (l + 1))
                for n in range(24):
                    key = (l, "mod", n)
                    bk = reader(dve, key)
                    for a in range(2):
                        ins = nc.vector.tensor_scalar(modc[:, 2 * n + a, :], bk[:, 2 * a:2 * a + 2],
                                                      modraw[:, 2 * n + a:2 * n + a + 1], None, ALU.add)
                    freed(dve, ins, key, True)
                for gs, m, g in ((gs1, 1, G_N1), (gs2, 4, G_N2)):
                    for s in range(2):
                        link(nc.vector.scalar_tensor_tensor(out=gs[:, s, :], in0=modc[:, 8 * m:8 * m + 8, s], scalar=1.0,
                                                            in1=gains[:, g:g + 8], op0=ALU.add, op1=ALU.mult))
                for t in range(6):
                    link(nc.vector.tensor_copy(g2t[:, t, :], modc[:, 40:48, 1 if t < 2 else 0]))
                dve.sem_inc(mod_done, 1)
                norm(l, "n1", segs(l, True))
                run_items(na_items(l))
                run_units(na_units(l))
                barrier(dve, stage_no(l, 1))
                run_items(latent_items(l))
                for grp in range(2):
                    run_items(head_items(l, grp))
                    run_units(mla_units(l, grp))
                    barrier(dve, stage_no(l, 2 + grp))
                nt = len(tiles(l))
                dve.wait_ge(bsb_in, 16 * (l + 1))
                for i in range(nt + 1):
                    if i < nt:
                        t = tiles(l)[i]
                        cnt["sg"] += 1
                        dve.wait_ge(sg_rt, cnt["sg"])
                        link(nc.vector.reciprocal(stats[:, i % 4, 5:6], stats[:, i % 4, 7:8]))
                        nc.vector.tensor_scalar(vg[:, t, :], vg[:, t, :], stats[:, i % 4, 5:6], None,
                                                ALU.mult).then_inc(sg_v, 1)
                    if i >= 1:
                        t = tiles(l)[i - 1]
                        key = (l, "mix", t)
                        bk = reader(dve, key)
                        for g in range(GROUPS):
                            ins = nc.vector.scalar_tensor_tensor(
                                out=sgtmp[:, 1, g * P:(g + 1) * P], in0=bk[:, g * P:(g + 1) * P],
                                scalar=gains[:, G_SG + g:G_SG + g + 1], in1=bsb[:, g, :], op0=ALU.mult, op1=ALU.add)
                        freed(dve, ins, key, True)
                        link(nc.vector.tensor_tensor(uT[:, :, t * P:(t + 1) * P], uT[:, :, t * P:(t + 1) * P],
                                                     sgtmp[:, 1, :].rearrange("p (g q) -> p g q", g=4), ALU.mult))
                barrier(dve, stage_no(l, 4))
                n_sig = 0
                for b in range(3):
                    for ch in range(8):
                        for s0, n in segs(l):
                            cnt["sig"] += 1
                            dve.wait_ge(sig_ready, cnt["sig"])
                            key = (l, "b", b, ch, s0)
                            bk = reader(dve, key)
                            dst = merged[:, ch, s0:s0 + n] if b == 0 else prod[:, n_sig % 2, 0:n]
                            freed(dve, nc.vector.tensor_tensor(dst, bk[:, 0:n], sig[:, n_sig % 3, 0:n], ALU.mult), key, True)
                            if b:
                                m = merged[:, ch, s0:s0 + n]
                                link(nc.vector.tensor_tensor(m, m, dst, ALU.add))
                            n_sig += 1
                dve.sem_inc(merged_ready, 1)
                for ch in range(8):
                    for s0, n in segs(l):
                        key = (l, "o", ch, s0)
                        bk = reader(dve, key)
                        s = 1 if s0 == 0 else 0
                        xx = X[:, ch, s0:s0 + n]
                        freed(dve, nc.vector.scalar_tensor_tensor(out=xx, in0=bk[:, 0:n], scalar=modc[:, 16 + ch, s:s + 1],
                                                                  in1=xx, op0=ALU.mult, op1=ALU.add), key, True)
                dve.sem_inc(x_ready, 1)
                norm(l, "n2", segs(l))
                barrier(dve, stage_no(l, 5))
                key = (l, "kT")
                bk = reader(dve, key)
                freed(dve, nc.vector.tensor_copy(kT, bk[:, 0:256].rearrange("p (r t) -> p r t", r=2)), key, True)
                dve.sem_inc(kt_copied, 1)
                for t in tiles(l):
                    for half in range(2):
                        key = (l, "h2", t, half)
                        bk = reader(dve, key)
                        freed(dve, nc.vector.tensor_copy(h2tok[:, t, half * 512:(half + 1) * 512], bk), key)
                for cc in range(16):
                    for g, tt in enumerate((tiles(l)[:4], tiles(l)[4:])):
                        if tt:
                            key = (l, "sc", cc, g)
                            bk = reader(dve, key)
                            w = len(tt)
                            dst = scores[:, 0:48 * 256].rearrange("p (t c k) -> p t c k", t=6, k=P)[:, tt[0]:tt[0] + w, cc, :]
                            freed(dve, nc.vector.tensor_copy(dst, bk[:, 0:w * P].rearrange("p (t k) -> p t k", k=P)), key)
                barrier(dve, stage_no(l, 6))
                t0, t1 = PEER_TILES(l)
                nt = t1 - t0
                unit0 = 0 if l == 0 else 48
                tile0 = 0 if l == 0 else 6

                def one(ins, s):
                    ins.then_inc(dve_chain, 1)
                    s[0] += 1
                    dve.wait_ge(dve_chain, s[1] + s[0])
                    dve.sem_inc(dve_go, 1)

                def topk_steps(s, src, uo, slot, best_ev, exp_ev):
                    steps = []

                    def half_steps(a):
                        x_, v_, i_ = sc[:, a, :], topv[:, a, :], topi[:, a, :]
                        steps.append(lambda: (one(nc.vector.max(v_[:, 0:8], x_), s),
                                              one(nc.vector.max_index(i_[:, 0:8], v_[:, 0:8], x_), s)))
                        steps.append(lambda: (one(nc.vector.match_replace(wk, v_[:, 0:8], x_, NEG), s),
                                              one(nc.vector.max(v_[:, 8:16], wk), s),
                                              one(nc.vector.max_index(i_[:, 8:16], v_[:, 8:16], wk), s)))
                    steps.append(lambda: one(nc.vector.tensor_copy(sc, src), s))
                    half_steps(0)
                    half_steps(1)
                    c3 = cand.rearrange("p (k j) -> p k j", k=16)
                    steps.append(lambda: (
                        one(nc.vector.tensor_copy(topif, topi[:, :, :]), s),
                        one(nc.vector.tensor_tensor(c3, topv[:, 0, :].unsqueeze(2).broadcast_to([P, 16, 16]),
                                                    topv[:, 1, :].unsqueeze(1).broadcast_to([P, 16, 16]), ALU.add), s)))
                    steps.append(lambda: (
                        (dve.wait_ge(exp_gate, exp_ev - 1) if exp_ev is not None else None),
                        dve.sem_inc(dve_go, 1),
                        one(nc.vector.max(best[:, 0:8], cand), s),
                        one(nc.vector.max_index(pos[:, 0:8], best[:, 0:8], cand), s)))
                    steps.append(lambda: (
                        one(nc.vector.match_replace(cwk, best[:, 0:8], cand, NEG), s),
                        one(nc.vector.max(best[:, 8:16], cwk), s),
                        one(nc.vector.max_index(pos[:, 8:16], best[:, 8:16], cwk), s)))
                    steps.append(lambda: (
                        nc.vector.tensor_scalar(nbest, best[:, 0:1], -1.0, None, ALU.mult).then_inc(best_ready, 1),
                        nc.vector.tensor_single_scalar(dig[:, 0, :], pos[:, :], 4, ALU.logical_shift_right),
                        one(nc.vector.tensor_single_scalar(dig[:, 1, :], pos[:, :], 15, ALU.bitwise_and), s),
                        one(nc.vector.tensor_copy(digit, dig[:, :, :]), s)))
                    for a in range(2):
                        steps.append(lambda a=a: (
                            one(nc.vector.tensor_tensor(oh, iota16, digit[:, a, :].unsqueeze(2).broadcast_to([P, 16, 16]),
                                                        ALU.is_equal), s),
                            one(nc.vector.tensor_tensor(oh, oh, topif[:, a, :].unsqueeze(1).broadcast_to([P, 16, 16]),
                                                        ALU.mult), s),
                            one(nc.vector.tensor_reduce(expert[:, a, :], oh, axis=AX.X, op=ALU.add), s)))
                    steps.append(lambda: (
                        one(nc.vector.scalar_tensor_tensor(out=expert[:, 0, :], in0=expert[:, 0, :], scalar=float(PK),
                                                           in1=expert[:, 1, :], op0=ALU.mult, op1=ALU.add), s),
                        nc.vector.tensor_scalar(idx[:, slot, :], expert[:, 0, :], float(l * NEXP), None,
                                                ALU.add).then_inc(idx_ready, 1)))
                    return steps

                def unit_src(tu):
                    return scores[:, bass.ds(tu * 256, 256)].rearrange("p (a k) -> p a k", a=2)

                def dot(j, ur, r, uw):
                    dve.wait_ge(u_full[ur], uw)
                    nc.vector.tensor_tensor_reduce(out=ub[:, ur, :], in0=ub[:, ur, :], in1=h2cur, scale=1.0, scalar=0.0,
                                                   op0=ALU.mult, op1=ALU.add, accum_out=dots[:, r, j:j + 1]).then_inc(u_used, 1)

                s = [0, chain[0]]
                nc.vector.memset(zrow, 0.0)
                one(nc.vector.tensor_copy(h2cur, h2tok[:, t0, :]), s)
                dve.sem_inc(zero_done, 1)
                for f in topk_steps(s, unit_src(8 * t0), 0, 0, unit0 + 1, None):
                    f()
                st1 = topk_steps(s, unit_src(8 * t0 + 1), 1, 1, unit0 + 2, unit0 + 2)
                for k in range(16):
                    dot(k, k % 8, 0, unit0 * 32 + 16 * (k // 8 + 1))
                    if k < len(st1):
                        st1[k]()
                dve.wait_ge(exp_gate, unit0 + 1)
                one(nc.vector.reciprocal(grcp, gsum[:, 0:1]), s)
                one(nc.vector.tensor_scalar(gate[:, 0, :], gate[:, 0, :], grcp, None, ALU.mult), s)
                chain[0] += s[0]

                def peer_tile(t, last, s):
                    tu = t * 8 + unit0
                    one(nc.vector.tensor_copy(g2cur, g2t[:, bass.ds(t + t0, 1), :].rearrange("p a k -> p (a k)")), s)
                    for j in range(8):
                        has_u = not (last and j == 7)
                        has_k = not (last and j >= 6)
                        dve.wait_ge(gel_ready, tu + (j + 1))
                        nc.vector.tensor_tensor(wgt[:, j % 2, :], gel[:, j % 2, :], gate[:, j % 4, :],
                                                ALU.mult).then_inc(wgt_ready, 1)
                        steps = topk_steps(s, unit_src(t * 8 + (8 * t0 + j + 2)), None, (j + 2) % 4, tu + (j + 3),
                                           tu + (j + 3)) if has_k else []
                        if has_u:
                            dve.wait_ge(exp_gate, tu + (j + 2))
                            one(nc.vector.reciprocal(grcp, gsum[:, (j + 1) % 4:(j + 1) % 4 + 1]), s)
                            one(nc.vector.tensor_scalar(gate[:, (j + 1) % 4, :], gate[:, (j + 1) % 4, :], grcp, None,
                                                        ALU.mult), s)
                            if j == 7:
                                one(nc.vector.tensor_copy(h2cur, h2tok[:, bass.ds(t + (t0 + 1), 1), :]
                                                          .rearrange("p a d -> p (a d)")), s)
                            for k in range(16):
                                dot(k, k % 8, (j + 1) % 2, tu * 32 + (32 * (j + 1) + 16 * (k // 8 + 1)))
                                if k < len(steps):
                                    steps[k]()
                        assert len(steps) <= 16
                    dve.wait_ge(outT_done, t + (tile0 + 1))
                    for k in range(DK):
                        xx = X[:, k, bass.ds(t * P + t0 * P, P)]
                        nc.vector.scalar_tensor_tensor(out=xx, in0=banks[:, 2 + k // 4, (k % 4) * P:(k % 4 + 1) * P],
                                                       scalar=g2cur[:, k:k + 1], in1=xx, op0=ALU.mult,
                                                       op1=ALU.add).then_inc(outT_added, 1)
                    dve.wait_ge(outT_added, t * DK + (tile0 * DK + DK))

                s = [0, chain[0]]
                peer_tile(0, nt == 1, s)
                per_tile = s[0]
                chain[0] += per_tile
                if nt > 2:
                    with dve.Fori(1, nt - 1) as t:
                        s = [0, (t - 1) * per_tile + chain[0]]
                        peer_tile(t, False, s)
                        assert s[0] == per_tile
                    chain[0] += (nt - 2) * per_tile
                s = [0, chain[0]]
                peer_tile(nt - 1, True, s)
                chain[0] += s[0]
                dve.sem_inc(x_ready, 1)
                barrier(dve, stage_no(l, 7))

        @block.gpsimd
        def _(pool):
            pool.memset(epsc[:, :], EPS).then_inc(eps_ready, 1)
            flat = na_rpb.rearrange("l h r c -> (l h r c)")
            pool.dma_start(rpb_pad[PAD:PAD + LAYERS * NBIAS], flat).then_inc(pad_in, 16)
            pool.dma_start(rpb_pad[0:PAD], flat[0:PAD]).then_inc(pad_in, 16)
            pool.dma_start(rpb_pad[PAD + LAYERS * NBIAS:], flat[0:PAD]).then_inc(pad_in, 16)
            pool.wait_ge(pad_in, 48)
            for l in range(LAYERS):
                for y in range(3):
                    for i in range(COL_BLK):
                        src = bass.AP(rpb_pad.tensor, PAD + l * NBIAS + BIAS_SHIFT[y] - i,
                                      [[CO * RO, HEADS], [CO, RO], [1, KEY_COLS]])
                        dst = bass.AP(rpb_rows.tensor, ((l * HEADS * 3 + y) * COL_BLK + i) * RO * KEY_COLS,
                                      [[3 * COL_BLK * RO * KEY_COLS, HEADS], [KEY_COLS, RO], [1, KEY_COLS]])
                        pool.dma_start(dst, src).then_inc(rows_made, 16)
            pool.wait_ge(rows_made, 16 * LAYERS * 3 * COL_BLK)
            pool.wait_ge(const_in, 16)

            def bias_head(l, h):
                if h >= 2:
                    b, use = jobs[(l, "na", h - 2, NBLK - 1, "s", 0)]
                    pool.wait_ge(bank_free[b], use + 1)
                for r in range(ROWS):
                    src = rpb_rows[l, h, :, :, (7 - r) * KEY_COLS:(7 - r + ROWS) * KEY_COLS].rearrange("y i k -> i y k")
                    pool.dma_start(bias[r * COL_BLK:(r + 1) * COL_BLK, h % 2, :, 0:NLOC], src).then_inc(bias_in, 16)
                pool.wait_ge(bias_in, 16 * ROWS * (HEADS * l + h + 1))
                bb = bias[:, h % 2, :, 0:NLOC]
                pool.tensor_tensor(bb, bb, masks.rearrange("p (y k) -> p y k", y=3), ALU.add).then_inc(bias_ready, 1)

            for l in range(LAYERS):
                b, use = jobs[(l, "n1", CTX)]
                pool.wait_ge(bank_full[b], use + 1)
                pool.memset(bias[:, :, :, NLOC:512], 0.0).then_inc(bias_zero, 1)
                pool.wait_ge(bias_zero, l + 1)
                bias_head(l, 0)
                bias_head(l, 1)
                pool.wait_ge(v_copied, l + 1)
                for n in range(NBLK):
                    start = min(max(n * COL_BLK - WIN_C // 2, 0), GRID_W - KEY_COLS)
                    for cch in range(2):
                        for r in range(4):
                            row = 4 * cch + r
                            p0 = (row % 2) * GRID_W + start
                            pool.dma_start(vblk[32 * r:32 * r + 32, n, cch, :],
                                           vna[p0:p0 + 32, 2 + row // 2, :]).then_inc(vblk_in, 16)
                for h in range(2, HEADS):
                    bias_head(l, h)
                barrier(pool, stage_no(l, 1))
                pool.wait_ge(rope_done, 9 * l + 1)
                for hh in range(4):
                    pool.tensor_copy(km[64:96, hh, :], krT[64:96, :]).then_inc(kr_copied, 1)
                for grp in range(2):
                    barrier(pool, stage_no(l, 2 + grp))
                pool.dma_start(bsb, sg_b[l:l + 1].rearrange("l g q -> l (g q)").broadcast_to([P, GROUPS * P])
                               .rearrange("p (g q) -> p g q", g=GROUPS)).then_inc(bsb_in, 16)
                pool.wait_ge(bsb_in, 16 * (l + 1))
                for k in (4, 5, 6):
                    barrier(pool, stage_no(l, k))
                t0, t1 = PEER_TILES(l)
                nt = t1 - t0
                unit0 = 0 if l == 0 else 48

                def gather(table, buf, sems, slot, col):
                    pool.indirect_dma_start(buf[:, slot, :], None, table,
                                            bass.IndirectOffsetOnAxis(ap=col, axis=0)).then_inc(sems[slot], 16)

                pool.wait_ge(idx_ready, unit0 + 1)
                for k in range(16):
                    if k >= U_RING or unit0:
                        pool.wait_ge(u_used, unit0 * 16 + k - U_RING + 1)
                    gather(u_rows, ub, u_full, k % U_RING, idx[:, 0, k:k + 1])

                def peer_tile(t, last, first):
                    for j in range(8):
                        for k in range(16):
                            g = j * 16 + k
                            if not (last and j == 7):
                                if k == 0:
                                    pool.wait_ge(idx_ready, t * 8 + (unit0 + j + 2))
                                    pool.sem_inc(pool_go, 1)
                                pool.wait_ge(u_used, t * 128 + (unit0 * 16 + g + 16 - U_RING + 1))
                                pool.sem_inc(pool_go, 1)
                                gather(u_rows, ub, u_full, k % U_RING, idx[:, (j + 1) % 4, k:k + 1])
                            if not (first and g < V_RING and not unit0):
                                pool.wait_ge(v_used, t * 128 + (unit0 * 16 + g - V_RING + 1))
                                pool.sem_inc(pool_go, 1)
                            gather(v_rows, vb, v_full, k % V_RING, idx[:, j % 4, k:k + 1])

                peer_tile(0, nt == 1, True)
                if nt > 2:
                    with pool.Fori(1, nt - 1) as t:
                        peer_tile(t, False, False)
                peer_tile(nt - 1, True, False)
                barrier(pool, stage_no(l, 7))

        @block.sync
        def _(sp):
            sp.dma_start(consts[:, :], const).then_inc(const_in, 16)
            sp.dma_start(cT[:, :, :], cond).then_inc(c_in, 16)

            def smalls(l):
                sp.dma_start(modraw[:, :], columns[l, :, 0:48]).then_inc(small_in, 16)
                sp.dma_start(gains[:, :], columns[l, :, 48:80]).then_inc(small_in, 16)

            def weights(n):
                name, parts = loads[n]
                s = n % W_SLOTS
                if n >= W_SLOTS:
                    b, use = jobs[last_use[loads[n - W_SLOTS][0]]]
                    sp.wait_ge(bank_full[b], use + 1)
                for off, src in parts:
                    shape = src.shape
                    if len(shape) == 3:
                        dst = wring[:, s, off:off + shape[1] * shape[2]].rearrange("p (k n) -> p k n", k=shape[1])
                    else:
                        dst = wring[:, s, off:off + shape[1]]
                    sp.dma_start(dst, src).then_inc(w_full[s], 16)

            n_layer = len(loads) // LAYERS
            for l in range(LAYERS):
                for n in range(l * n_layer, (l + 1) * n_layer):
                    if n == l * n_layer + 4:
                        if l:
                            sp.wait_ge(stage_end, 4 * stage_no(0, 6))
                        smalls(l)
                        if l == 0:
                            for t in range(6):
                                for half in range(2):
                                    src = (ctx_in[:, 4 * half:4 * half + 4, t * P:(t + 1) * P] if t < 2 else
                                           x[:, 4 * half:4 * half + 4, (t - 2) * P:(t - 1) * P])
                                    sp.dma_start(X[:, 4 * half:4 * half + 4, t * P:(t + 1) * P], src).then_inc(x_in, 16)
                    weights(n)
            sp.wait_ge(x_ready, 2 * LAYERS)
            sp.dma_start(out, X[:, :, CTX:T]).then_inc(out_in, 16)
            sp.wait_ge(out_in, 16)


_NAMES = ['x', 'ctx', 'w_mod', 'w_in', 'na_rpb', 'sg_w', 'sg_b', 'mla_w_uq', 'mla_w_uk', 'mla_w_uv', 'w_branch', 'w_out',
          'peer_w_q', 'peer_k1', 'peer_k2', 'peer_u', 'peer_v']


def as_columns(inputs):
    def chunks(name):
        a = np.asarray(inputs[name])
        return a.reshape(LAYERS, -1, P).transpose(0, 2, 1)

    def stacked(*names):
        rows = [np.asarray(inputs[n]) if n else np.zeros((LAYERS, 64), np.float32) for n in names]
        a = np.concatenate(rows, axis=1)
        return np.pad(a, ((0, 0), (0, P - a.shape[1])))[:, :, None]

    return np.concatenate([chunks('b_mod'), chunks('g_norm1'), chunks('g_norm2'), stacked('na_g_q', 'na_g_q'),
                           stacked('na_g_k', 'na_g_k'), chunks('sg_g'), chunks('mla_g_cq'), chunks('mla_g_ckv'),
                           stacked('mla_g_qn', 'mla_g_qr'), stacked('mla_g_kn'), stacked(None, 'mla_g_kr'),
                           np.zeros((LAYERS, P, 4), np.float32)], axis=2)


def kernel(**inputs):
    import numpy as _np
    import concourse.bacc as _bacc
    from concourse import mybir as _mybir
    from concourse.bass_utils import run_bass_kernel_spmd as _run

    nc = _bacc.Bacc("TRN2", target_bir_lowering=False, num_devices=1)
    arrays, args = {}, []

    def feed(name, a):
        a = _np.ascontiguousarray(a)
        arrays[name] = a
        args.append(nc.dram_tensor(name, a.shape, _mybir.dt.from_np(a.dtype), kind="ExternalInput").ap())

    for name in _NAMES:
        a = _np.asarray(inputs[name])
        if name in ("x", "ctx"):
            a = a[0].T.reshape(D // P, P, -1).transpose(1, 0, 2)
        feed(f"in_{name}_dram", a)
    pair = _np.stack([_np.asarray(inputs['c'])[0], _np.asarray(inputs['c_ctx'])], axis=-1)
    feed("cond_dram", pair.reshape(D // P, P, 2).transpose(1, 0, 2))
    feed("columns_dram", as_columns(inputs))
    feed("const_dram", constants())
    args.append(nc.dram_tensor("out_0_dram", (P, D // P, SEQ), _mybir.dt.float32, kind="ExternalOutput").ap())
    program(nc, *args)
    r = _run(nc, [arrays], core_ids=[0])
    o = r.results[0]["out_0_dram"]
    return o.transpose(2, 1, 0).reshape(1, SEQ, D)
```

```python
import concourse.bass as bass
from concourse import mybir
from contextlib import ExitStack
import numpy as np

P = 128
D, SEQ, CTX, LAYERS = 1024, 512, 256, 2
T = CTX + SEQ
DK = D // P
EPS = 1e-6
GRID_W, ROWS = 64, SEQ // 64
HEADS, HD = 8, 64
NA_W = HEADS * HD
WIN_R, WIN_C, KEY_COLS, COL_BLK = 8, 16, 32, 16
NBLK = GRID_W // COL_BLK
NLOC = ROWS * KEY_COLS
Q_RANK, KV_RANK, ROPE, QK = 256, 128, 32, 96
SG_W, GROUPS = 512, 4
C_Q, C_K, C_V = 0, NA_W, 2 * NA_W
C_CQ = 3 * NA_W
C_CKV = C_CQ + Q_RANK
C_U = C_CKV + KV_RANK + ROPE
C_SV = C_U + SG_W
C_GATE = C_SV + SG_W
PH, PK, TOPK, NEXP = 8, 128, 16, 128 * 128
RO, CO = 2 * WIN_R - 1, 2 * WIN_C - 1
BIAS_SHIFT = [15, 7, -1]
KIND = [0, 1, 1, 2]
W_SLOTS, W_LEN = 4, 2048
NEG = -3.0e38
U_RING, V_RING = 8, 4
IDX_RING = 4


def constants():
    f = np.float32
    ident = np.eye(P, dtype=f)
    ones = np.full((P, P), 1.0 / D, f)
    blk = np.zeros((P, P), f)
    blk[:64, :64] = blk[64:, 64:] = 1.0 / 64
    blkq = np.zeros((P, P), f)
    blkq[:64, :64] = 1.0 / 64
    blkq[64:96, 64:96] = 1.0 / 32
    rot = np.zeros((P, P), f)
    for j in range(16):
        rot[80 + j, 64 + j] = -1.0
        rot[64 + j, 80 + j] = 1.0
    t = np.arange(SEQ)
    nf = ROPE // 4
    inv = (np.float32(10000.0) ** (-np.arange(nf, dtype=f) / np.float32(nf))).astype(f)
    ang = np.concatenate([(t // GRID_W).astype(f)[:, None] * inv, (t % GRID_W).astype(f)[:, None] * inv], -1)
    cs = np.zeros((P, 2, SEQ), f)
    for a in (64, 80):
        cs[a:a + 16, 0] = np.cos(ang).T
        cs[a:a + 16, 1] = np.sin(ang).T
    mask = np.zeros((P, 3, KEY_COLS), f)
    for kind, blkno in ((0, 0), (1, 1), (2, 3)):
        start = min(max(blkno * COL_BLK - WIN_C // 2, 0), GRID_W - KEY_COLS)
        for i in range(COL_BLK):
            qc = blkno * COL_BLK + i
            ws = min(max(qc - WIN_C // 2, 0), GRID_W - WIN_C)
            bad = [j for j in range(KEY_COLS) if not ws <= start + j < ws + WIN_C]
            for r in range(ROWS):
                mask[r * COL_BLK + i, kind, bad] = -1e30
    iota = np.tile(np.arange(16, dtype=f)[None, None, :], (P, 16, 1))
    return np.concatenate([ident, ones, blk, blkq, rot, cs.reshape(P, -1), mask.reshape(P, -1),
                           iota.reshape(P, -1)], axis=1)


N_CONST = 5 * P + 2 * SEQ + 3 * KEY_COLS + 256


def program(nc, x, ctx_in, na_bias, sg_w, sg_b, mla_w_uk, mla_w_uv, peer_k1, peer_k2, peer_u, peer_v,
            w_mod, w_qkv, w_cq, w_ckv, w_uq, w_sg, w_gate, w_branch, w_out, peer_w_q, cond, columns, const, out):
    F, U32 = mybir.dt.float32, mybir.dt.uint32
    ALU, ACT, AX = mybir.AluOpType, mybir.ActivationFunctionType, mybir.AxisListType
    u_rows = peer_u.rearrange("l e d -> (l e) d")
    v_rows = peer_v.rearrange("l e d -> (l e) d")

    with ExitStack() as stack:
        def sb(name, shape, dt=F):
            return stack.enter_context(nc.sbuf_tensor(name, shape, dt))

        def sem(name):
            return stack.enter_context(nc.semaphore(name))

        X = sb("X", [P, DK, T])
        consts = sb("consts", [P, N_CONST])
        o = 0
        ident = consts[:, 0:P]
        ones = consts[:, P:2 * P]
        blk64 = consts[:, 2 * P:3 * P]
        blkq = consts[:, 3 * P:4 * P]
        rot = consts[:, 4 * P:5 * P]
        o = 5 * P
        cosT = consts[:, o:o + SEQ]
        sinT = consts[:, o + SEQ:o + 2 * SEQ]
        o += 2 * SEQ
        masks = consts[:, o:o + 3 * KEY_COLS]
        o += 3 * KEY_COLS
        iota16 = consts[:, o:o + 256].rearrange("p (k j) -> p k j", k=16)

        smalls = sb("smalls", [P, LAYERS, 80])
        modraw = [smalls[:, l, 0:48] for l in range(LAYERS)]
        gain_of = [smalls[:, l, 48:80] for l in range(LAYERS)]
        modcs = sb("modc", [P, LAYERS, 48, 2])
        modc_of = [modcs[:, l] for l in range(LAYERS)]
        G_N1, G_N2, G_Q, G_K, G_SG, G_CQ, G_CKV, G_QQ, G_KN, G_KR = 0, 8, 16, 17, 18, 22, 24, 25, 26, 27
        gs1 = sb("gs1", [P, 2, DK])
        gs2 = sb("gs2", [P, 2, DK])
        epsc = sb("epsc", [P, 1])
        cT = sb("cT", [P, DK, 2])
        modrow = sb("modrow", [P, 2, 256])
        cS = sb("cS", [P, DK, 2])
        stats = sb("stats", [P, 4, 8])
        g2t = sb("g2t", [P, 6, DK])
        idx = sb("idx", [P, IDX_RING, TOPK], U32)
        gate = sb("gate", [P, IDX_RING, TOPK])
        dots = sb("dots", [P, 2, TOPK])
        gel = sb("gel", [P, 2, TOPK])
        wgt = sb("wgt", [P, 2, TOPK])

        wring = sb("wring", [P, W_SLOTS, W_LEN])
        R_LEN = 35600
        region = sb("region", [P, R_LEN])

        def at(off, n):
            assert off + n <= R_LEN
            return region[:, off:off + n]

        hT = at(0, DK * T).rearrange("p (k t) -> p k t", k=DK)
        R1 = DK * T
        R1_LEN = 13312
        naq = at(R1, 3072).rearrange("p (c t) -> p c t", c=4)
        nak = at(R1 + 3072, 3072).rearrange("p (c t) -> p c t", c=4)
        vna = at(R1 + 6144, 3072).rearrange("p (t f) -> p t f", t=6)
        vblk = at(R1 + 9216, 4096).rearrange("p (n c f) -> p n c f", n=NBLK, c=2)
        cqT = at(R1, 1536).rearrange("p (c t) -> p c t", c=2)
        ckvT = at(R1 + 1536, T)
        krT = at(R1 + 2304, T)
        vm = at(R1 + 3072, 3072).rearrange("p (t f) -> p t f", t=6)
        qm = at(R1 + 6144, 3072).rearrange("p (h t) -> p h t", h=4)
        km = at(R1 + 9216, 3072).rearrange("p (h t) -> p h t", h=4)
        uT = at(R1, 3072).rearrange("p (c t) -> p c t", c=4)
        vg = at(R1 + 3072, 3072).rearrange("p (t f) -> p t f", t=6)
        wsT = at(R1 + 6144, 512).rearrange("p (g q) -> p g q", g=4)
        bsb = at(R1 + 6656, 512).rearrange("p (g q) -> p g q", g=4)
        merged = at(R1 + 7168, DK * T).rearrange("p (k t) -> p k t", k=DK)
        B1 = R1 + R1_LEN
        aT = at(B1, 3072).rearrange("p (c t) -> p c t", c=4)
        mT = at(B1 + 3072, 3072).rearrange("p (c t) -> p c t", c=4)
        S0 = B1 + 6144
        sqn = at(S0, 4096)
        rn = at(S0 + 4096, 512)
        bias = at(S0, 3072).rearrange("p (b y k) -> p b y k", b=2, y=3)
        pr = at(S0 + 3072, 2304).rearrange("p (r k) -> p r k", r=3)
        ptr = at(S0 + 5376, 1536).rearrange("p (r k) -> p r k", r=2)
        sq = at(S0 + 3072, 3072).rearrange("p (r a k) -> p r a k", r=3, a=2)
        rr = at(S0 + 6912, 1536).rearrange("p (r k) -> p r k", r=3)
        sig = at(S0, 1536).rearrange("p (r k) -> p r k", r=3)
        prod = at(S0 + 1536, 1024).rearrange("p (r k) -> p r k", r=2)
        sgtmp = at(S0 + 2560, 1024).rearrange("p (r k) -> p r k", r=2)
        ub = at(0, U_RING * D).rearrange("p (r d) -> p r d", r=U_RING)
        vb = at(U_RING * D, V_RING * D).rearrange("p (r d) -> p r d", r=V_RING)
        qr = at(8192, 2 * T).rearrange("p (r t) -> p r t", r=2)
        kT = at(8192 + 2 * T, 256).rearrange("p (r t) -> p r t", r=2)
        o = 12288
        h2tok = at(o, 6 * D).rearrange("p (t d) -> p t d", t=6)
        o += 6 * D
        scores = at(o, 48 * 256)
        o += 48 * 256
        h2cur = at(o, D)
        tokout = at(o + D, D).rearrange("p (k q) -> p k q", k=DK)
        o += 2 * D
        dg = at(o, 256).rearrange("p (r q) -> p r q", r=2)
        sc = at(o + 256, 256).rearrange("p (a k) -> p a k", a=2)
        wk = at(o + 512, P)
        topv = at(o + 640, 32).rearrange("p (a k) -> p a k", a=2)
        topif = at(o + 672, 32).rearrange("p (a k) -> p a k", a=2)
        cand = at(o + 704, 256)
        cwk = at(o + 960, 256)
        oh = at(o + 1216, 256).rearrange("p (k j) -> p k j", k=16)
        best = at(o + 1472, 16)
        digit = at(o + 1488, 32).rearrange("p (a k) -> p a k", a=2)
        expert = at(o + 1520, 32).rearrange("p (a k) -> p a k", a=2)
        nbest = at(o + 1552, 1)
        gsum = at(o + 1553, IDX_RING)
        g2cur = at(o + 1560, DK)
        grcp = at(o + 1568, 1)
        zrow = at(o + 1570, P)
        topi = at(o + 1700, 32).bitcast(U32).rearrange("p (a k) -> p a k", a=2)
        pos = at(o + 1732, 16).bitcast(U32)
        dig = at(o + 1748, 32).bitcast(U32).rearrange("p (a k) -> p a k", a=2)

        banks = stack.enter_context(nc.psum_tensor("banks", [P, 8, 512], F))

        bank_full = [sem(f"bank_full{b}") for b in range(8)]
        bank_free = [sem(f"bank_free{b}") for b in range(8)]
        w_full = [sem(f"w_full{s}") for s in range(W_SLOTS)]
        const_in = sem("const_in")
        x_in = sem("x_in")
        c_in = sem("c_in")
        c_done = sem("c_done")
        small_in = sem("small_in")
        mod_done = sem("mod_done")
        modrow_ready = sem("modrow_ready")
        sq_ready = sem("sq_ready")
        rt_ready = sem("rt_ready")
        xn_ready = sem("xn_ready")
        h_ready = sem("h_ready")
        nsq_ready = sem("nsq_ready")
        nrt_ready = sem("nrt_ready")
        item_done = sem("item_done")
        v_copied = sem("v_copied")
        vblk_in = sem("vblk_in")
        bias_in = sem("bias_in")
        bias_ready = sem("bias_ready")
        bias_zero = sem("bias_zero")
        eps_ready = sem("eps_ready")
        rope_done = sem("rope_done")
        bsb_in = sem("bsb_in")
        s_biased = sem("s_biased")
        neg_max = sem("neg_max")
        exp_done = sem("exp_done")
        p_ready = sem("p_ready")
        pt_ready = sem("pt_ready")
        kr_copied = sem("kr_copied")
        stage_end = sem("stage_end")
        sg_sq = sem("sg_sq")
        sg_rt = sem("sg_rt")
        sg_v = sem("sg_v")
        ws_ready = sem("ws_ready")
        sig_ready = sem("sig_ready")
        merged_ready = sem("merged_ready")
        x_ready = sem("x_ready")
        q_copied = sem("q_copied")
        kt_copied = sem("kt_copied")
        dve_chain = sem("dve_chain")
        act_chain = sem("act_chain")
        u_full = [sem(f"u_full{s}") for s in range(U_RING)]
        v_full = [sem(f"v_full{s}") for s in range(V_RING)]
        u_used = sem("u_used")
        v_used = sem("v_used")
        idx_ready = sem("idx_ready")
        best_ready = sem("best_ready")
        exp_gate = sem("exp_gate")
        gel_ready = sem("gel_ready")
        wgt_ready = sem("wgt_ready")
        diag_ready = sem("diag_ready")
        acc_start = sem("acc_start")
        acc_done = sem("acc_done")
        acc_copied = sem("acc_copied")
        outT_done = sem("outT_done")
        outT_added = sem("outT_added")
        pool_go = sem("pool_go")
        dve_go = sem("dve_go")
        zero_done = sem("zero_done")
        out_in = sem("out_in")

        jobs = {}
        last_use = {}
        loads = []
        load_at = {}

        def bank(b):
            return banks[:, b, :]

        SEG_CTX, SEG_LAT = (0, CTX), (CTX, SEQ)

        def segs(l, keys=False):
            return [SEG_CTX, SEG_LAT] if (l == 0 or keys) else [SEG_LAT]

        def tiles(l, keys=False):
            return list(range(6)) if (l == 0 or keys) else list(range(2, 6))

        def add_load(name, parts):
            load_at[name] = len(loads)
            loads.append((name, parts))

        def plan_mod(l, ns):
            for n in ns:
                add_load((l, "mod", n), [(0, w_mod[l, n])])

        def plan_loads(l):
            if l == 0:
                plan_mod(0, MOD_FIRST)
            for n, what in enumerate(("v", "q", "k")):
                for half in range(2):
                    add_load((l, what, half), [(0, w_qkv[l, 2 * n + half])])
            if l == 0:
                plan_mod(0, MOD_REST)
            add_load((l, "cq", 0), [(0, w_cq[l, 0])])
            add_load((l, "ckv", 0), [(0, w_ckv[l, 0])])
            add_load((l, "uk", 0), [(0, mla_w_uk[l]), (512, mla_w_uv[l])])
            add_load((l, "uq", 0), [(0, w_uq[l, 0])])
            for n, what in enumerate(("u", "sv")):
                for half in range(2):
                    add_load((l, what, half), [(0, w_sg[l, 2 * n + half])])
            add_load((l, "sgw", 0), [(0, sg_w[l].rearrange("g p q -> p g q"))])
            for b in range(3):
                for half in range(2):
                    add_load((l, "wb", b, half), [(0, w_branch[l, b, half])])
                    for q in range(2):
                        add_load((l, "gt", b, half, q), [(0, w_gate[l, 4 * b + 2 * half + q])])
                    if l == 0:
                        plan_mod(1, MOD_NEXT(b, half))
            for q in range(4):
                add_load((l, "wo", q), [(0, w_out[l, q])])
            add_load((l, "pk", 0), [(0, peer_k1[l]), (128, peer_k2[l])])
            for q in range(8):
                add_load((l, "pq", q), [(0, peer_w_q[l, q])])

        MOD_FIRST, MOD_REST = range(8), range(8, 24)

        def MOD_NEXT(b, half):
            return range(4 * (2 * b + half), 4 * (2 * b + half) + 4)

        for l in range(LAYERS):
            plan_loads(l)

        def w_value(name):
            n = load_at[name]
            return n % W_SLOTS, 16 * sum(len(loads[m][1]) for m in range(n % W_SLOTS, n + 1, W_SLOTS))

        def na_items(l):
            out_ = []
            for what, dest, g, keys in (("q", naq, G_Q, False), ("k", nak, G_K, True)):
                for ch in range(4):
                    for s0, n in segs(l, keys):
                        out_.append(dict(key=(l, what, ch, s0), load=(l, what, ch // 2), s0=s0, n=n, p0=0, p1=P,
                                         raw=[[("h", k, k * 256 + (ch % 2) * P, P) for k in range(DK)]],
                                         norm=blk64, scale=1.0, gain=[g], dest=[dest[:, ch, s0:s0 + n]], rope=None))
            return out_

        def latent_items(l):
            out_ = []
            for s0, n in segs(l):
                out_.append(dict(key=(l, "cq", s0), load=(l, "cq", 0), s0=s0, n=n, p0=0, p1=P,
                                 raw=[[("h", k, k * 256 + a * P, P) for k in range(DK)] for a in range(2)],
                                 norm=ones, scale=4.0, gain=[G_CQ, G_CQ + 1],
                                 dest=[cqT[:, a, s0:s0 + n] for a in range(2)], rope=None))
            for s0, n in segs(l, True):
                out_.append(dict(key=(l, "ckv", s0), load=(l, "ckv", 0), s0=s0, n=n, p0=0, p1=P,
                                 raw=[[("h", k, k * 160, P) for k in range(DK)]],
                                 norm=ones, scale=8.0, gain=[G_CKV], dest=[ckvT[:, s0:s0 + n]], rope=None))
            for s0, n in segs(l, True):
                out_.append(dict(key=(l, "kr", s0), load=(l, "ckv", 0), s0=s0, n=n, p0=64, p1=96,
                                 raw=[[("h", k, k * 160 + P, ROPE) for k in range(DK)]],
                                 norm=blkq, scale=1.0, gain=[G_KR], dest=[krT[64:96, s0:s0 + n]],
                                 rope=krT[64:96, s0:s0 + n] if s0 else None))
            return out_

        def head_items(l, grp):
            out_ = []
            for hh in range(4):
                h = 4 * grp + hh
                for s0, n in segs(l):
                    out_.append(dict(key=(l, "mq", h, s0), load=(l, "uq", 0), s0=s0, n=n, p0=0, p1=QK,
                                     raw=[[("cq", k, k * 768 + h * QK, QK) for k in range(2)]],
                                     norm=blkq, scale=1.0, gain=[G_QQ], dest=[qm[0:QK, hh, s0:s0 + n]],
                                     rope=qm[64:96, hh, s0:s0 + n] if s0 else None))
                for s0, n in segs(l, True):
                    out_.append(dict(key=(l, "mk", h, s0), load=(l, "uk", 0), s0=s0, n=n, p0=0, p1=64,
                                     raw=[[("ckv", 0, h * 64, 64)]],
                                     norm=blk64, scale=1.0, gain=[G_KN], dest=[km[0:64, hh, s0:s0 + n]], rope=None))
            return out_

        def na_units(l):
            out_ = []
            for h in range(HEADS):
                p0 = 64 * (h % 2)
                qh, kh = naq[p0:p0 + 64, h // 2, :], nak[p0:p0 + 64, h // 2, :]
                fcols = slice(64 * h, 64 * h + 64)
                ah = aT[p0:p0 + 64, h // 2, :]
                for n in range(NBLK):
                    start = min(max(n * COL_BLK - WIN_C // 2, 0), GRID_W - KEY_COLS)
                    grid_k = kh[:, CTX:T].rearrange("p (r w) -> p r w", w=GRID_W)[:, :, start:start + KEY_COLS]
                    grid_a = ah[:, CTX:T].rearrange("p (r w) -> p r w", w=GRID_W)[:, :, n * COL_BLK:(n + 1) * COL_BLK]
                    out_.append(dict(key=(l, "na", h, n), pieces=[512], q=qh[:, CTX + n * P:CTX + (n + 1) * P],
                                     k=[(0, 0, NLOC, grid_k), (0, NLOC, 512, kh[:, 0:CTX])],
                                     bias=(h, KIND[n]), scale=0.125, po=p0,
                                     v=[vblk[:, n, 0, fcols], vblk[:, n, 1, fcols], vna[:, 0, fcols], vna[:, 1, fcols]],
                                     dest=grid_a))
            if l == 0:
                for h in range(HEADS):
                    p0 = 64 * (h % 2)
                    for t in range(2):
                        out_.append(dict(key=(l, "nac", h, t), pieces=[CTX],
                                         q=naq[p0:p0 + 64, h // 2, t * P:(t + 1) * P],
                                         k=[(0, 0, CTX, nak[p0:p0 + 64, h // 2, 0:CTX])], bias=None, scale=0.125, po=p0,
                                         v=[vna[:, a, 64 * h:64 * h + 64] for a in range(2)],
                                         dest=aT[p0:p0 + 64, h // 2, t * P:(t + 1) * P]))
            return out_

        def mla_units(l, grp):
            out_ = []
            for hh in range(4):
                h = 4 * grp + hh
                p0 = 64 * (h % 2)
                for t in tiles(l):
                    nk = T if t >= 2 else CTX
                    pieces = [512, 256] if nk == T else [256]
                    ks = [(a, 0, w, km[0:QK, hh, 512 * a:512 * a + w]) for a, w in enumerate(pieces)]
                    out_.append(dict(key=(l, "mla", h, t), pieces=pieces, q=qm[0:QK, hh, t * P:(t + 1) * P], k=ks,
                                     bias=None, scale=float(QK) ** -0.5, po=p0,
                                     v=[vm[:, a, 64 * h:64 * h + 64] for a in range(nk // P)],
                                     dest=mT[p0:p0 + 64, h // 2, t * P:(t + 1) * P]))
            return out_

        block = stack.enter_context(nc.Block())

        def barrier(eng, n):
            eng.drain().then_inc(stage_end, 1)
            eng.wait_ge(stage_end, 4 * n)

        def stage_no(l, k):
            return 6 * l + k

        def PEER_TILES(l):
            return (0, 6) if l == 0 else (2, 6)

        @block.tensor
        def _(pe):
            cnt = dict(sq=0, nsq=0, item=0, p=0, pt=0, rope=0, mod=0)

            def fill(key):
                j = len(jobs)
                b, use = j % 8, j // 8
                jobs[key] = (b, use)
                if use:
                    pe.wait_ge(bank_free[b], use)
                return bank(b)

            def filled(ins, key):
                ins.then_inc(bank_full[jobs[key][0]], 1)

            def weights(name, key):
                s, v = w_value(name)
                pe.wait_ge(w_full[s], v)
                last_use[name] = key
                return wring[:, s, :]

            def mod_rows(l, n):
                key = (l, "modr", n)
                bk = fill(key)
                w = weights((l, "mod", n), key)
                for k in range(DK):
                    ins = nc.tensor.matmul(bk[0:2, 0:256], cS[:, k, :], w[:, k * 256:(k + 1) * 256],
                                           start=(k == 0), stop=(k == DK - 1))
                filled(ins, key)

            def mod_turn(l, n):
                key = (l, "mod", n)
                bk = fill(key)
                cnt["mod"] += 1
                pe.wait_ge(modrow_ready, cnt["mod"])
                for a in range(2):
                    ins = nc.tensor.transpose(bk[:, 2 * a:2 * a + 2], modrow[0:2, n % 2, a * P:(a + 1) * P], ident[0:2, 0:2])
                filled(ins, key)

            def mod_jobs(l, ns):
                for n in ns:
                    mod_rows(l, n)
                    if n > ns[0]:
                        mod_turn(l, n - 1)
                mod_turn(l, ns[-1])

            def norm_sum(l, which, i, s0, n):
                key = (l, which, s0)
                bk = fill(key)
                cnt["nsq"] += 1
                pe.wait_ge(nsq_ready, cnt["nsq"])
                for k in range(DK):
                    ins = nc.tensor.matmul(bk[:, 0:n], ones, sqn[:, k * n:(k + 1) * n], start=(k == 0), stop=(k == DK - 1))
                filled(ins, key)

            def moving(kind, k, s0, n):
                if kind == "h":
                    return hT[:, k, s0:s0 + n]
                return cqT[:, k, s0:s0 + n] if kind == "cq" else ckvT[:, s0:s0 + n]

            def run_items(items):
                base = cnt["item"]
                for i in range(len(items) + 4):
                    if i < len(items):
                        it = items[i]
                        for a, terms in enumerate(it["raw"]):
                            key = it["key"] + ("raw", a)
                            bk = fill(key)
                            w = weights(it["load"], key)
                            for m, (kind, k, wo, wn) in enumerate(terms):
                                ins = nc.tensor.matmul(bk[it["p0"]:it["p1"], 0:it["n"]], w[:, wo:wo + wn],
                                                       moving(kind, k, it["s0"], it["n"]),
                                                       start=(m == 0), stop=(m == len(terms) - 1))
                            filled(ins, key)
                    if 2 <= i < len(items) + 2:
                        it = items[i - 2]
                        key = it["key"] + ("norm",)
                        bk = fill(key)
                        cnt["sq"] += 1
                        pe.wait_ge(sq_ready, cnt["sq"])
                        p0, p1 = it["p0"], it["p1"]
                        na = len(it["raw"])
                        for a in range(na):
                            ins = nc.tensor.matmul(bk[p0:p1, 0:it["n"]], it["norm"][p0:p1, p0:p1],
                                                   sq[p0:p1, (i - 2) % 3, a, 0:it["n"]], start=(a == 0), stop=(a == na - 1))
                        filled(ins, key)
                    if i >= 4 and items[i - 4]["rope"] is not None:
                        it = items[i - 4]
                        key = it["key"] + ("rope",)
                        bk = fill(key)
                        pe.wait_ge(item_done, base + i - 3)
                        ins = nc.tensor.matmul(bk[64:96, 0:it["n"]], rot[64:96, 64:96], it["rope"], start=True, stop=True)
                        filled(ins, key)
                cnt["item"] = base + len(items)
                pe.wait_ge(item_done, cnt["item"])
                cnt["rope"] += sum(it["rope"] is not None for it in items)
                if cnt["rope"]:
                    pe.wait_ge(rope_done, cnt["rope"])

            def run_units(units, extras={}):
                for i in range(len(units) + 3):
                    if i < len(units):
                        un = units[i]
                        for a, w in enumerate(un["pieces"]):
                            key = un["key"] + ("s", a)
                            bk = fill(key)
                            for pa, c0, c1, kk in un["k"]:
                                if pa == a:
                                    ins = nc.tensor.matmul(bk[:, c0:c1], un["q"], kk, start=True, stop=True)
                            filled(ins, key)
                    if i in extras:
                        extras[i]()
                    if 2 <= i < len(units) + 2:
                        un = units[i - 2]
                        cnt["p"] += 1
                        pe.wait_ge(p_ready, cnt["p"])
                        for a, w in enumerate(un["pieces"]):
                            key = un["key"] + ("t", a)
                            bk = fill(key)
                            for j in range(w // P):
                                ins = nc.tensor.transpose(bk[:, j * P:(j + 1) * P],
                                                          pr[:, (i - 2) % 3, 512 * a + j * P:512 * a + (j + 1) * P], ident)
                            filled(ins, key)
                    if 3 <= i:
                        un = units[i - 3]
                        key = un["key"] + ("o",)
                        bk = fill(key)
                        cnt["pt"] += 1
                        pe.wait_ge(pt_ready, cnt["pt"])
                        nv = len(un["v"])
                        for j, vv in enumerate(un["v"]):
                            ins = nc.tensor.matmul(bk[un["po"]:un["po"] + 64, 0:P], vv, ptr[:, (i - 3) % 2, j * P:(j + 1) * P],
                                                   start=(j == 0), stop=(j == nv - 1))
                        filled(ins, key)

            def between(l):
                return {6 * m: (lambda n=n: mod_jobs(0, range(n, n + 2))) for m, n in enumerate(MOD_REST[::2])} if l == 0 else {}

            def feature_job(key, load, wo, s0, n, terms=DK, step=256, src=None):
                bk = fill(key)
                w = weights(load, key)
                src = hT if src is None else src
                for k in range(terms):
                    ins = nc.tensor.matmul(bk[:, 0:n], w[:, k * step + wo:k * step + wo + P], src[:, k, s0:s0 + n],
                                           start=(k == 0), stop=(k == terms - 1))
                filled(ins, key)

            pe.wait_ge(const_in, 16)
            hcount = 0
            for l in range(LAYERS):
                if l == 0:
                    pe.wait_ge(c_done, 1)
                    mod_jobs(0, MOD_FIRST)
                for i, (s0, n) in enumerate(segs(l, True)):
                    norm_sum(l, "n1", i, s0, n)
                for half in range(2):
                    for t in tiles(l, True):
                        if half == 0 and t in (0, 2):
                            hcount += 1
                            pe.wait_ge(h_ready, hcount)
                        key = (l, "v", half, t)
                        bk = fill(key)
                        w = weights((l, "v", half), key)
                        for k in range(DK):
                            ins = nc.tensor.matmul(bk[:, 0:256], hT[:, k, t * P:(t + 1) * P], w[:, k * 256:(k + 1) * 256],
                                                   start=(k == 0), stop=(k == DK - 1))
                        filled(ins, key)
                run_items(na_items(l))
                pe.wait_ge(vblk_in, 16 * 32 * (l + 1))
                run_units(na_units(l), between(l))
                barrier(pe, stage_no(l, 1))
                run_items(latent_items(l))
                for t in tiles(l, True):
                    key = (l, "vm", t)
                    bk = fill(key)
                    w = weights((l, "uk", 0), key)
                    filled(nc.tensor.matmul(bk, ckvT[:, t * P:(t + 1) * P], w[:, 512:1024], start=True, stop=True), key)
                for grp in range(2):
                    run_items(head_items(l, grp))
                    pe.wait_ge(kr_copied, 4 * (l + 1))
                    run_units(mla_units(l, grp))
                barrier(pe, stage_no(l, 2))
                for ch in range(4):
                    for s0, n in segs(l):
                        feature_job((l, "u", ch, s0), (l, "u", ch // 2), (ch % 2) * P, s0, n)
                for half in range(2):
                    for t in tiles(l):
                        key = (l, "sv", half, t)
                        bk = fill(key)
                        w = weights((l, "sv", half), key)
                        for k in range(DK):
                            ins = nc.tensor.matmul(bk[:, 0:256], hT[:, k, t * P:(t + 1) * P], w[:, k * 256:(k + 1) * 256],
                                                   start=(k == 0), stop=(k == DK - 1))
                        filled(ins, key)
                key = (l, "wsT")
                bk = fill(key)
                w = weights((l, "sgw", 0), key)
                for g in range(GROUPS):
                    ins = nc.tensor.transpose(bk[:, g * P:(g + 1) * P], w[:, g * P:(g + 1) * P], ident)
                filled(ins, key)
                pe.wait_ge(ws_ready, l + 1)
                for i, t in enumerate(tiles(l)):
                    key = (l, "mix", t)
                    bk = fill(key)
                    pe.wait_ge(sg_v, (0 if l == 0 else 6) + i + 1)
                    for g in range(GROUPS):
                        ins = nc.tensor.matmul(bk[:, g * P:(g + 1) * P], vg[:, t, g * P:(g + 1) * P], wsT[:, g, :],
                                               start=True, stop=True)
                    filled(ins, key)
                barrier(pe, stage_no(l, 3))
                src = [aT, uT, mT]
                for b in range(3):
                    for ch in range(8):
                        half, q = ch // 4, (ch % 4) // 2
                        for s0, n in segs(l):
                            feature_job((l, "g", b, ch, s0), (l, "gt", b, half, q), (ch % 2) * P, s0, n)
                            feature_job((l, "b", b, ch, s0), (l, "wb", b, half), (ch % 4) * P, s0, n, 4, 512, src[b])
                        if l == 0 and ch % 4 == 3:
                            mod_jobs(1, MOD_NEXT(b, half))
                pe.wait_ge(merged_ready, l + 1)
                for ch in range(8):
                    for s0, n in segs(l):
                        feature_job((l, "o", ch, s0), (l, "wo", ch // 2), (ch % 2) * P, s0, n, src=merged)
                for i, (s0, n) in enumerate(segs(l)):
                    norm_sum(l, "n2", i, s0, n)
                hcount += len(segs(l))
                pe.wait_ge(h_ready, hcount)
                barrier(pe, stage_no(l, 4))
                key = (l, "kT")
                bk = fill(key)
                w = weights((l, "pk", 0), key)
                for a in range(2):
                    ins = nc.tensor.transpose(bk[:, a * P:(a + 1) * P], w[:, a * P:(a + 1) * P], ident)
                filled(ins, key)
                pe.wait_ge(kt_copied, l + 1)
                for t in tiles(l):
                    for half in range(2):
                        key = (l, "h2", t, half)
                        bk = fill(key)
                        for j in range(4):
                            ins = nc.tensor.transpose(bk[:, j * P:(j + 1) * P], hT[:, 4 * half + j, t * P:(t + 1) * P], ident)
                        filled(ins, key)
                ns = len(segs(l))
                for ch in range(17):
                    if ch < 16:
                        for s0, n in segs(l):
                            feature_job((l, "pq", ch, s0), (l, "pq", ch // 2), (ch % 2) * P, s0, n)
                    if ch >= 1:
                        cc = ch - 1
                        pe.wait_ge(q_copied, (32 * l) + ns * (cc + 1))
                        for g, tt in enumerate((tiles(l)[:4], tiles(l)[4:])):
                            if tt:
                                key = (l, "sc", cc, g)
                                bk = fill(key)
                                for j, t in enumerate(tt):
                                    ins = nc.tensor.matmul(bk[:, j * P:(j + 1) * P], qr[:, cc % 2, t * P:(t + 1) * P],
                                                           kT[:, cc % 2, :], start=True, stop=True)
                                filled(ins, key)
                nj = len(jobs)
                for b in range(8):
                    pe.wait_ge(bank_free[b], (nj - b + 7) // 8)
                barrier(pe, stage_no(l, 5))
                t0, t1 = PEER_TILES(l)
                done_tiles = 0 if l == 0 else 6
                pe.wait_ge(zero_done, l + 1)
                with pe.Fori(0, t1 - t0) as t:
                    tile = t + done_tiles
                    for a in range(2):
                        nc.tensor.matmul(bank(a), zrow, consts[:, 0:512], start=True, stop=False, skip_group_check=True)
                    for j in range(128):
                        pe.wait_ge(diag_ready, tile * 128 + (j + 1))
                        pe.wait_ge(v_full[j % V_RING], tile * (16 * 128 // V_RING) + 16 * (j // V_RING + 1))
                        for a in range(2):
                            ins = nc.tensor.matmul(bank(a), dg[:, j % 2, :], vb[:, j % V_RING, a * 512:(a + 1) * 512],
                                                   start=False, stop=(j == 127), skip_group_check=True)
                        ins.then_inc(v_used, 1)
                    pe.wait_ge(acc_copied, tile * 2 + 2)
                    for k in range(DK):
                        ins = nc.tensor.transpose(banks[:, 2 + k // 4, (k % 4) * P:(k % 4 + 1) * P], tokout[:, k, :], ident)
                    ins.then_inc(outT_done, 1)
                    pe.wait_ge(outT_added, tile * DK + DK)
                barrier(pe, stage_no(l, 6))

        def reader(eng, key):
            b, use = jobs[key]
            eng.wait_ge(bank_full[b], use + 1)
            return bank(b)

        def freed(eng, ins, key, wait=False):
            b, use = jobs[key]
            ins.then_inc(bank_free[b], 1)
            if wait:
                eng.wait_ge(bank_free[b], use + 1)

        @block.scalar
        def _(act):
            chain = [0]
            cnt = dict(sqn=0, nrt=0, xn=0, sq=0, item=0, neg=0, sb_=0, exp=0, u=0, sgv=0)

            def link(ins):
                chain[0] += 1
                ins.then_inc(act_chain, 1)
                act.wait_ge(act_chain, chain[0])

            def mod_copies(l, ns):
                for n in ns:
                    if n >= ns[0] + 2:
                        b, use = jobs[(l, "mod", n - 2)]
                        act.wait_ge(bank_full[b], use + 1)
                    key = (l, "modr", n)
                    bk = reader(act, key)
                    freed(act, nc.scalar.activation(modrow[0:2, n % 2, :], bk[0:2, 0:256], ACT.Copy), key, True)
                    act.sem_inc(modrow_ready, 1)

            def norm(l, which, sg_list):
                for s0, n in sg_list:
                    if x_val[0]:
                        act.wait_ge(x_ready, x_val[0])
                    if last_norm[0] is not None:
                        b, use = jobs[last_norm[0]]
                        act.wait_ge(bank_full[b], use + 1)
                    nc.scalar.activation(sqn[:, 0:DK * n].rearrange("p (k t) -> p k t", k=DK), X[:, :, s0:s0 + n],
                                         ACT.Square).then_inc(nsq_ready, 1)
                    key = (l, which, s0)
                    last_norm[0] = key
                    bk = reader(act, key)
                    if cnt["nrt"]:
                        act.wait_ge(xn_ready, cnt["xn"])
                    freed(act, nc.scalar.activation(rn[:, 0:n], bk[:, 0:n], ACT.Sqrt, bias=epsc[:, 0:1]), key, True)
                    act.sem_inc(nrt_ready, 1)
                    cnt["nrt"] += 1
                    gs, sh = (gs1, 0) if which == "n1" else (gs2, 3)
                    act.wait_ge(mod_done, 2 * l + (1 if which == "n1" else 2))
                    strm = 1 if s0 == 0 else 0
                    for k in range(DK):
                        cnt["xn"] += 1
                        act.wait_ge(xn_ready, cnt["xn"])
                        ins = nc.scalar.activation(hT[:, k, s0:s0 + n], hT[:, k, s0:s0 + n], ACT.Identity,
                                                   scale=gs[:, strm, k:k + 1], bias=modc_of[l][:, 8 * sh + k, strm:strm + 1])
                    ins.then_inc(h_ready, 1)

            def run_items(items):
                for i in range(len(items) + 2):
                    if i < len(items):
                        it = items[i]
                        p0, p1 = it["p0"], it["p1"]
                        if i >= 3:
                            b, use = jobs[items[i - 3]["key"] + ("norm",)]
                            act.wait_ge(bank_full[b], use + 1)
                        for a in range(len(it["raw"])):
                            bk = reader(act, it["key"] + ("raw", a))
                            ins = nc.scalar.activation(sq[p0:p1, i % 3, a, 0:it["n"]], bk[p0:p1, 0:it["n"]], ACT.Square)
                        ins.then_inc(sq_ready, 1)
                    if i >= 2:
                        it = items[i - 2]
                        p0, p1 = it["p0"], it["p1"]
                        key = it["key"] + ("norm",)
                        bk = reader(act, key)
                        if i >= 5:
                            act.wait_ge(item_done, cnt["item"] + i - 4)
                        freed(act, nc.scalar.activation(rr[p0:p1, (i - 2) % 3, 0:it["n"]], bk[p0:p1, 0:it["n"]],
                                                        ACT.Sqrt, scale=it["scale"], bias=epsc[p0:p1, 0:1]), key)
                cnt["item"] += len(items)

            def run_units(units, extras={}):
                u0 = cnt["u"]
                for i in range(len(units) + 3):
                    if i < len(units):
                        un = units[i]
                        cnt["neg"] += 1
                        act.wait_ge(neg_max, cnt["neg"])
                        st = stats[:, i % 4, :]
                        if i >= 3 and un["bias"] is None:
                            b, use = jobs[units[i - 3]["key"] + ("t", len(units[i - 3]["pieces"]) - 1)]
                            act.wait_ge(bank_full[b], use + 1)
                        for a, w in enumerate(un["pieces"]):
                            dst = pr[:, i % 3, 512 * a:512 * a + w]
                            if un["bias"] is not None:
                                ins = nc.scalar.activation(dst, dst, ACT.Exp, bias=st[:, 2:3], accum_out=st[:, 4 + a:5 + a])
                                ins.then_inc(exp_done, 1)
                                cnt["exp"] += 1
                            else:
                                key = un["key"] + ("s", a)
                                bk = reader(act, key)
                                freed(act, nc.scalar.activation(dst, bk[:, 0:w], ACT.Exp, bias=st[:, 2:3],
                                                                accum_out=st[:, 4 + a:5 + a]), key)
                    if i in extras:
                        extras[i]()
                    if 2 <= i < len(units) + 2:
                        un = units[i - 2]
                        if i >= 4:
                            b, use = jobs[units[i - 4]["key"] + ("o",)]
                            act.wait_ge(bank_full[b], use + 1)
                        for a, w in enumerate(un["pieces"]):
                            key = un["key"] + ("t", a)
                            bk = reader(act, key)
                            freed(act, nc.scalar.activation(ptr[:, (i - 2) % 2, 512 * a:512 * a + w], bk[:, 0:w], ACT.Copy),
                                  key, a == len(un["pieces"]) - 1)
                        act.sem_inc(pt_ready, 1)
                    if 3 <= i:
                        un = units[i - 3]
                        key = un["key"] + ("o",)
                        bk = reader(act, key)
                        po = un["po"]
                        src = bk[po:po + 64, 0:P]
                        if len(un["dest"].shape) == 3:
                            src = src.rearrange("p (r w) -> p r w", w=COL_BLK)
                        freed(act, nc.scalar.activation(un["dest"], src, ACT.Copy), key)
                cnt["u"] += len(units)

            last_norm = [None]
            x_val = [0]
            act.wait_ge(c_in, 16)
            link(nc.scalar.activation(cS[:, :, :], cT[:, :, :], ACT.Sigmoid))
            mod_copies(0, MOD_FIRST)
            act.wait_ge(x_in, 16 * 2)
            act.wait_ge(eps_ready, 1)
            for l in range(LAYERS):
                norm(l, "n1", segs(l, True))
                for half in range(2):
                    for t in tiles(l, True):
                        key = (l, "v", half, t)
                        bk = reader(act, key)
                        freed(act, nc.scalar.activation(vna[:, t, half * 256:(half + 1) * 256], bk[:, 0:256], ACT.Copy), key, True)
                act.sem_inc(v_copied, 1)
                run_items(na_items(l))
                run_units(na_units(l), {6 * m: (lambda n=n: mod_copies(0, range(n, n + 2)))
                                        for m, n in enumerate(MOD_REST[::2])} if l == 0 else {})
                barrier(act, stage_no(l, 1))
                run_items(latent_items(l))
                for t in tiles(l, True):
                    key = (l, "vm", t)
                    bk = reader(act, key)
                    freed(act, nc.scalar.activation(vm[:, t, :], bk, ACT.Copy), key)
                for grp in range(2):
                    run_items(head_items(l, grp))
                    run_units(mla_units(l, grp))
                barrier(act, stage_no(l, 2))
                for ch in range(4):
                    for s0, n in segs(l):
                        key = (l, "u", ch, s0)
                        bk = reader(act, key)
                        freed(act, nc.scalar.activation(uT[:, ch, s0:s0 + n], bk[:, 0:n], ACT.Gelu_apprx_tanh), key)
                for half in range(2):
                    for t in tiles(l):
                        key = (l, "sv", half, t)
                        bk = reader(act, key)
                        freed(act, nc.scalar.activation(vg[:, t, half * 256:(half + 1) * 256], bk[:, 0:256],
                                                        ACT.Gelu_apprx_tanh), key, True)
                key = (l, "wsT")
                bk = reader(act, key)
                freed(act, nc.scalar.activation(wsT, bk.rearrange("p (g q) -> p g q", g=4), ACT.Copy), key, True)
                act.sem_inc(ws_ready, 1)
                for i, t in enumerate(tiles(l)):
                    link(nc.scalar.activation(sgtmp[:, 0, :], vg[:, t, :], ACT.Square, accum_out=stats[:, i % 4, 6:7]))
                    cnt["sgv"] += 1
                    if i >= 4:
                        act.wait_ge(sg_v, cnt["sgv"] - 4)
                    link(nc.scalar.activation(stats[:, i % 4, 7:8], stats[:, i % 4, 6:7], ACT.Sqrt, scale=1.0 / SG_W,
                                              bias=epsc[:, 0:1]))
                    act.sem_inc(sg_rt, 1)
                barrier(act, stage_no(l, 3))
                n_sig, sig_hist = 0, []
                for b in range(3):
                    for ch in range(8):
                        for s0, n in segs(l):
                            key = (l, "g", b, ch, s0)
                            bk = reader(act, key)
                            if n_sig >= 3:
                                kb, ku = jobs[sig_hist[n_sig - 3]]
                                act.wait_ge(bank_free[kb], ku + 1)
                            sig_hist.append((l, "b", b, ch, s0))
                            freed(act, nc.scalar.activation(sig[:, n_sig % 3, 0:n], bk[:, 0:n], ACT.Sigmoid), key, True)
                            act.sem_inc(sig_ready, 1)
                            n_sig += 1
                        if l == 0 and ch % 4 == 3:
                            mod_copies(1, MOD_NEXT(b, ch // 4))
                x_val[0] = 2 * l + 1
                norm(l, "n2", segs(l))
                barrier(act, stage_no(l, 4))
                for ch in range(16):
                    for s0, n in segs(l):
                        key = (l, "pq", ch, s0)
                        bk = reader(act, key)
                        if ch >= 2:
                            g = 1 if l == 0 else 0
                            b, use = jobs[(l, "sc", ch - 2, g)]
                            act.wait_ge(bank_full[b], use + 1)
                        freed(act, nc.scalar.activation(qr[:, ch % 2, s0:s0 + n], bk[:, 0:n], ACT.Copy), key, True)
                        act.sem_inc(q_copied, 1)
                barrier(act, stage_no(l, 5))
                t0, t1 = PEER_TILES(l)
                nt = t1 - t0
                unit0 = 0 if l == 0 else 48
                tile0 = 0 if l == 0 else 6

                def exp_best(e):
                    ev, slot = e
                    act.wait_ge(best_ready, ev)
                    nc.scalar.activation(gate[:, slot, :], best, ACT.Exp, bias=nbest,
                                         accum_out=gsum[:, slot:slot + 1]).then_inc(exp_gate, 1)

                def gelu_dots(ev16, ev, r):
                    act.wait_ge(u_used, ev16)
                    act.activation(gel[:, r, :], dots[:, r, :], ACT.Gelu_apprx_tanh).then_inc(gel_ready, 1)

                exp_best((unit0 + 1, 0))
                exp_best((unit0 + 2, 1))
                gelu_dots(unit0 * 16 + 16, 0, 0)

                def peer_tile(t, last, first):
                    for j in range(8):
                        tu = t * 8 + unit0
                        for k in range(16):
                            if k == 0:
                                act.wait_ge(wgt_ready, tu + (j + 1))
                            if not (first and not unit0 and j == 0 and k < 2):
                                act.wait_ge(v_used, t * 128 + (unit0 * 16 + 16 * j + k - 1))
                            act.activation(dg[:, k % 2, :], ident, ACT.Copy, scale=wgt[:, j % 2, k:k + 1]).then_inc(diag_ready, 1)
                            if k == 13 and not (last and j >= 6):
                                exp_best((tu + (j + 3), (j + 2) % 4))
                        if not (last and j == 7):
                            gelu_dots(t * 128 + (unit0 * 16 + 16 * (j + 2)), 0, (j + 1) % 2)
                    for a in range(2):
                        if a == 0:
                            act.wait_ge(v_used, t * 128 + (unit0 * 16 + 128))
                        act.activation(tokout[:, 4 * a:4 * a + 4, :], bank(a).rearrange("p (k q) -> p k q", k=4),
                                       ACT.Copy).then_inc(acc_copied, 1)

                peer_tile(0, nt == 1, True)
                if nt > 2:
                    with act.Fori(1, nt - 1) as t:
                        peer_tile(t, False, False)
                peer_tile(nt - 1, True, False)
                x_val[0] = 2 * l + 2
                barrier(act, stage_no(l, 6))

        @block.vector
        def _(dve):
            chain = [0]
            cnt = dict(nrt=0, item=0, bias=0, exp=0, sg=0, sig=0)

            def link(ins):
                chain[0] += 1
                ins.then_inc(dve_chain, 1)
                dve.wait_ge(dve_chain, chain[0])

            def mod_columns(l, n):
                key = (l, "mod", n)
                bk = reader(dve, key)
                for a in range(2):
                    ins = nc.vector.tensor_scalar(modc_of[l][:, 2 * n + a, :], bk[:, 2 * a:2 * a + 2],
                                                  modraw[l][:, 2 * n + a:2 * n + a + 1], None, ALU.add)
                freed(dve, ins, key, True)

            def scaled_gain(l, gs, m, g):
                for s in range(2):
                    link(nc.vector.scalar_tensor_tensor(out=gs[:, s, :], in0=modc_of[l][:, 8 * m:8 * m + 8, s], scalar=1.0,
                                                        in1=gain_of[l][:, g:g + 8], op0=ALU.add, op1=ALU.mult))
                dve.sem_inc(mod_done, 1)

            def norm(l, which, sg_list):
                for s0, n in sg_list:
                    cnt["nrt"] += 1
                    dve.wait_ge(nrt_ready, cnt["nrt"])
                    link(nc.vector.reciprocal(rn[:, 0:n], rn[:, 0:n]))
                    for k in range(DK):
                        nc.vector.tensor_tensor(hT[:, k, s0:s0 + n], X[:, k, s0:s0 + n], rn[:, 0:n],
                                                ALU.mult).then_inc(xn_ready, 1)

            def run_items(items):
                gains = gain_of[items[0]["key"][0]]
                for i in range(len(items) + 2):
                    if i < len(items):
                        it = items[i]
                        p0, p1, n = it["p0"], it["p1"], it["n"]
                        b, use = jobs[it["key"] + ("norm",)]
                        dve.wait_ge(bank_free[b], use + 1)
                        link(nc.vector.reciprocal(rr[p0:p1, i % 3, 0:n], rr[p0:p1, i % 3, 0:n]))
                        for a, dst in enumerate(it["dest"]):
                            key = it["key"] + ("raw", a)
                            bk = reader(dve, key)
                            g = it["gain"][a]
                            if it["key"][1] == "q" and it["s0"]:
                                grid = bk[:, 0:SEQ].rearrange("p (r w) -> p r w", w=GRID_W)
                                root = rr[:, i % 3, :].rearrange("p (r w) -> p r w", w=GRID_W)
                                for m in range(NBLK):
                                    cols = slice(m * COL_BLK, (m + 1) * COL_BLK)
                                    ins = nc.vector.scalar_tensor_tensor(
                                        out=dst[:, m * P:(m + 1) * P].rearrange("p (r w) -> p r w", w=COL_BLK),
                                        in0=grid[:, :, cols], scalar=gains[:, g:g + 1], in1=root[:, :, cols],
                                        op0=ALU.mult, op1=ALU.mult)
                                freed(dve, ins, key, True)
                                continue
                            freed(dve, nc.vector.scalar_tensor_tensor(
                                out=dst, in0=bk[p0:p1, 0:n], scalar=gains[p0:p1, g:g + 1],
                                in1=rr[p0:p1, i % 3, 0:n], op0=ALU.mult, op1=ALU.mult), key, True)
                        dve.sem_inc(item_done, 1)
                    if i >= 2 and items[i - 2]["rope"] is not None:
                        it = items[i - 2]
                        r, n = it["rope"], it["n"]
                        key = it["key"] + ("rope",)
                        bk = reader(dve, key)
                        link(nc.vector.tensor_tensor(r, r, cosT[64:96, :], ALU.mult))
                        freed(dve, nc.vector.tensor_tensor(rtmp[64:96, 0:n], bk[64:96, 0:n], sinT[64:96, :], ALU.mult), key, True)
                        link(nc.vector.tensor_tensor(r, r, rtmp[64:96, 0:n], ALU.add))
                        dve.sem_inc(rope_done, 1)

            rtmp = at(S0, 512)

            def run_units(units, extras={}):
                for i in range(len(units) + 1):
                    if i < len(units):
                        un = units[i]
                        st = stats[:, i % 4, :]
                        if un["bias"] is not None:
                            h, kind = un["bias"]
                            if i >= 3:
                                b, use = jobs[units[i - 3]["key"] + ("t", len(units[i - 3]["pieces"]) - 1)]
                                dve.wait_ge(bank_full[b], use + 1)
                            key = un["key"] + ("s", 0)
                            bk = reader(dve, key)
                            dve.wait_ge(bias_ready, 8 * (un["key"][0]) + h + 1)
                            freed(dve, nc.vector.tensor_tensor(pr[:, i % 3, 0:512], bk, bias[:, h % 2, kind, :], ALU.add),
                                  key, True)
                            nc.vector.tensor_reduce(st[:, 2:3], pr[:, i % 3, 0:512], axis=AX.X, op=ALU.max,
                                                    negate=True).then_inc(neg_max, 1)
                        elif len(un["pieces"]) == 1:
                            bk = reader(dve, un["key"] + ("s", 0))
                            nc.vector.tensor_reduce(st[:, 2:3], bk[:, 0:un["pieces"][0]], axis=AX.X, op=ALU.max,
                                                    negate=True).then_inc(neg_max, 1)
                        else:
                            for a, w in enumerate(un["pieces"]):
                                bk = reader(dve, un["key"] + ("s", a))
                                ins = nc.vector.tensor_reduce(st[:, a:a + 1], bk[:, 0:w], axis=AX.X, op=ALU.max, negate=True)
                            link(ins)
                            nc.vector.tensor_tensor(st[:, 2:3], st[:, 0:1], st[:, 1:2], ALU.min).then_inc(neg_max, 1)
                    if i in extras:
                        extras[i]()
                    if 1 <= i:
                        un = units[i - 1]
                        st = stats[:, (i - 1) % 4, :]
                        npc = len(un["pieces"])
                        if un["bias"] is not None:
                            cnt["exp"] += 1
                            dve.wait_ge(exp_done, cnt["exp"])
                        else:
                            for a in range(npc):
                                b, use = jobs[un["key"] + ("s", a)]
                                dve.wait_ge(bank_free[b], use + 1)
                        if npc == 2:
                            link(nc.vector.tensor_tensor(st[:, 4:5], st[:, 4:5], st[:, 5:6], ALU.add))
                        link(nc.vector.reciprocal(st[:, 3:4], st[:, 4:5]))
                        w = sum(un["pieces"])
                        nc.vector.tensor_scalar(pr[:, (i - 1) % 3, 0:w], pr[:, (i - 1) % 3, 0:w], st[:, 3:4], None,
                                                ALU.mult).then_inc(p_ready, 1)

            dve.wait_ge(c_in, 16)
            dve.wait_ge(act_chain, 1)
            nc.vector.tensor_tensor(cS[:, :, :], cS[:, :, :], cT[:, :, :], ALU.mult).then_inc(c_done, 1)
            dve.wait_ge(small_in, 16)
            for l in range(LAYERS):
                link(nc.vector.tensor_scalar(gain_of[l][:, G_Q:G_Q + 1], gain_of[l][:, G_Q:G_Q + 1], 0.125, None, ALU.mult))
                link(nc.vector.tensor_scalar(gain_of[l][:, G_QQ:G_QQ + 1], gain_of[l][:, G_QQ:G_QQ + 1],
                                             float(QK) ** -0.5, None, ALU.mult))
            for l in range(LAYERS):
                gains, modc = gain_of[l], modc_of[l]
                if l == 0:
                    for n in MOD_FIRST:
                        mod_columns(0, n)
                scaled_gain(l, gs1, 1, G_N1)
                norm(l, "n1", segs(l, True))
                run_items(na_items(l))
                run_units(na_units(l), {6 * m: (lambda n=n: (mod_columns(0, n), mod_columns(0, n + 1)))
                                        for m, n in enumerate(MOD_REST[::2])} if l == 0 else {})
                barrier(dve, stage_no(l, 1))
                run_items(latent_items(l))
                for grp in range(2):
                    if grp:
                        b, use = jobs[mla_units(l, 0)[-1]["key"] + ("o",)]
                        dve.wait_ge(bank_free[b], use + 1)
                    run_items(head_items(l, grp))
                    run_units(mla_units(l, grp))
                barrier(dve, stage_no(l, 2))
                nt = len(tiles(l))
                dve.wait_ge(bsb_in, 16 * (l + 1))
                for i in range(nt + 1):
                    if i < nt:
                        t = tiles(l)[i]
                        cnt["sg"] += 1
                        dve.wait_ge(sg_rt, cnt["sg"])
                        link(nc.vector.reciprocal(stats[:, i % 4, 5:6], stats[:, i % 4, 7:8]))
                        nc.vector.tensor_scalar(vg[:, t, :], vg[:, t, :], stats[:, i % 4, 5:6], None,
                                                ALU.mult).then_inc(sg_v, 1)
                    if i >= 1:
                        t = tiles(l)[i - 1]
                        key = (l, "mix", t)
                        bk = reader(dve, key)
                        for g in range(GROUPS):
                            ins = nc.vector.scalar_tensor_tensor(
                                out=sgtmp[:, 1, g * P:(g + 1) * P], in0=bk[:, g * P:(g + 1) * P],
                                scalar=gains[:, G_SG + g:G_SG + g + 1], in1=bsb[:, g, :], op0=ALU.mult, op1=ALU.add)
                        freed(dve, ins, key, True)
                        link(nc.vector.tensor_tensor(uT[:, :, t * P:(t + 1) * P], uT[:, :, t * P:(t + 1) * P],
                                                     sgtmp[:, 1, :].rearrange("p (g q) -> p g q", g=4), ALU.mult))
                barrier(dve, stage_no(l, 3))
                scaled_gain(l, gs2, 4, G_N2)
                for t in range(6):
                    link(nc.vector.tensor_copy(g2t[:, t, :], modc[:, 40:48, 1 if t < 2 else 0]))
                n_sig = 0
                for b in range(3):
                    for ch in range(8):
                        for s0, n in segs(l):
                            cnt["sig"] += 1
                            dve.wait_ge(sig_ready, cnt["sig"])
                            key = (l, "b", b, ch, s0)
                            bk = reader(dve, key)
                            dst = merged[:, ch, s0:s0 + n] if b == 0 else prod[:, n_sig % 2, 0:n]
                            freed(dve, nc.vector.tensor_tensor(dst, bk[:, 0:n], sig[:, n_sig % 3, 0:n], ALU.mult), key, True)
                            if b:
                                m = merged[:, ch, s0:s0 + n]
                                link(nc.vector.tensor_tensor(m, m, dst, ALU.add))
                            n_sig += 1
                        if l == 0 and ch % 4 == 3:
                            for n in MOD_NEXT(b, ch // 4):
                                mod_columns(1, n)
                dve.sem_inc(merged_ready, 1)
                for ch in range(8):
                    for s0, n in segs(l):
                        key = (l, "o", ch, s0)
                        bk = reader(dve, key)
                        s = 1 if s0 == 0 else 0
                        xx = X[:, ch, s0:s0 + n]
                        freed(dve, nc.vector.scalar_tensor_tensor(out=xx, in0=bk[:, 0:n], scalar=modc[:, 16 + ch, s:s + 1],
                                                                  in1=xx, op0=ALU.mult, op1=ALU.add), key, True)
                dve.sem_inc(x_ready, 1)
                norm(l, "n2", segs(l))
                barrier(dve, stage_no(l, 4))
                key = (l, "kT")
                bk = reader(dve, key)
                freed(dve, nc.vector.tensor_copy(kT, bk[:, 0:256].rearrange("p (r t) -> p r t", r=2)), key, True)
                dve.sem_inc(kt_copied, 1)
                for t in tiles(l):
                    for half in range(2):
                        key = (l, "h2", t, half)
                        bk = reader(dve, key)
                        freed(dve, nc.vector.tensor_copy(h2tok[:, t, half * 512:(half + 1) * 512], bk), key)
                for cc in range(16):
                    for g, tt in enumerate((tiles(l)[:4], tiles(l)[4:])):
                        if tt:
                            key = (l, "sc", cc, g)
                            bk = reader(dve, key)
                            w = len(tt)
                            dst = scores[:, 0:48 * 256].rearrange("p (t c k) -> p t c k", t=6, k=P)[:, tt[0]:tt[0] + w, cc, :]
                            freed(dve, nc.vector.tensor_copy(dst, bk[:, 0:w * P].rearrange("p (t k) -> p t k", k=P)), key)
                barrier(dve, stage_no(l, 5))
                t0, t1 = PEER_TILES(l)
                nt = t1 - t0
                unit0 = 0 if l == 0 else 48
                tile0 = 0 if l == 0 else 6

                def one(ins, s):
                    ins.then_inc(dve_chain, 1)
                    s[0] += 1
                    dve.wait_ge(dve_chain, s[1] + s[0])
                    dve.sem_inc(dve_go, 1)

                def topk_steps(s, src, uo, slot, best_ev, exp_ev):
                    steps = []

                    def half_steps(a):
                        x_, v_, i_ = sc[:, a, :], topv[:, a, :], topi[:, a, :]
                        steps.append(lambda: (one(nc.vector.max(v_[:, 0:8], x_), s),
                                              one(nc.vector.max_index(i_[:, 0:8], v_[:, 0:8], x_), s)))
                        steps.append(lambda: (one(nc.vector.match_replace(wk, v_[:, 0:8], x_, NEG), s),
                                              one(nc.vector.max(v_[:, 8:16], wk), s),
                                              one(nc.vector.max_index(i_[:, 8:16], v_[:, 8:16], wk), s)))
                    steps.append(lambda: one(nc.vector.tensor_copy(sc, src), s))
                    half_steps(0)
                    half_steps(1)
                    c3 = cand.rearrange("p (k j) -> p k j", k=16)
                    steps.append(lambda: (
                        one(nc.vector.tensor_copy(topif, topi[:, :, :]), s),
                        one(nc.vector.tensor_tensor(c3, topv[:, 0, :].unsqueeze(2).broadcast_to([P, 16, 16]),
                                                    topv[:, 1, :].unsqueeze(1).broadcast_to([P, 16, 16]), ALU.add), s)))
                    steps.append(lambda: (
                        (dve.wait_ge(exp_gate, exp_ev - 1) if exp_ev is not None else None),
                        dve.sem_inc(dve_go, 1),
                        one(nc.vector.max(best[:, 0:8], cand), s),
                        one(nc.vector.max_index(pos[:, 0:8], best[:, 0:8], cand), s)))
                    steps.append(lambda: (
                        one(nc.vector.match_replace(cwk, best[:, 0:8], cand, NEG), s),
                        one(nc.vector.max(best[:, 8:16], cwk), s),
                        one(nc.vector.max_index(pos[:, 8:16], best[:, 8:16], cwk), s)))
                    steps.append(lambda: (
                        nc.vector.tensor_scalar(nbest, best[:, 0:1], -1.0, None, ALU.mult).then_inc(best_ready, 1),
                        nc.vector.tensor_single_scalar(dig[:, 0, :], pos[:, :], 4, ALU.logical_shift_right),
                        one(nc.vector.tensor_single_scalar(dig[:, 1, :], pos[:, :], 15, ALU.bitwise_and), s),
                        one(nc.vector.tensor_copy(digit, dig[:, :, :]), s)))
                    for a in range(2):
                        steps.append(lambda a=a: (
                            one(nc.vector.tensor_tensor(oh, iota16, digit[:, a, :].unsqueeze(2).broadcast_to([P, 16, 16]),
                                                        ALU.is_equal), s),
                            one(nc.vector.tensor_tensor(oh, oh, topif[:, a, :].unsqueeze(1).broadcast_to([P, 16, 16]),
                                                        ALU.mult), s),
                            one(nc.vector.tensor_reduce(expert[:, a, :], oh, axis=AX.X, op=ALU.add), s)))
                    steps.append(lambda: (
                        one(nc.vector.scalar_tensor_tensor(out=expert[:, 0, :], in0=expert[:, 0, :], scalar=float(PK),
                                                           in1=expert[:, 1, :], op0=ALU.mult, op1=ALU.add), s),
                        nc.vector.tensor_scalar(idx[:, slot, :], expert[:, 0, :], float(l * NEXP), None,
                                                ALU.add).then_inc(idx_ready, 1)))
                    return steps

                def unit_src(tu):
                    return scores[:, bass.ds(tu * 256, 256)].rearrange("p (a k) -> p a k", a=2)

                def dot(j, ur, r, uw):
                    dve.wait_ge(u_full[ur], uw)
                    nc.vector.tensor_tensor_reduce(out=ub[:, ur, :], in0=ub[:, ur, :], in1=h2cur, scale=1.0, scalar=0.0,
                                                   op0=ALU.mult, op1=ALU.add, accum_out=dots[:, r, j:j + 1]).then_inc(u_used, 1)

                s = [0, chain[0]]
                nc.vector.memset(zrow, 0.0)
                one(nc.vector.tensor_copy(h2cur, h2tok[:, t0, :]), s)
                dve.sem_inc(zero_done, 1)
                for f in topk_steps(s, unit_src(8 * t0), 0, 0, unit0 + 1, None):
                    f()
                st1 = topk_steps(s, unit_src(8 * t0 + 1), 1, 1, unit0 + 2, unit0 + 2)
                for k in range(16):
                    dot(k, k % 8, 0, unit0 * 32 + 16 * (k // 8 + 1))
                    if k < len(st1):
                        st1[k]()
                dve.wait_ge(exp_gate, unit0 + 1)
                one(nc.vector.reciprocal(grcp, gsum[:, 0:1]), s)
                one(nc.vector.tensor_scalar(gate[:, 0, :], gate[:, 0, :], grcp, None, ALU.mult), s)
                chain[0] += s[0]

                def peer_tile(t, last, s):
                    tu = t * 8 + unit0
                    one(nc.vector.tensor_copy(g2cur, g2t[:, bass.ds(t + t0, 1), :].rearrange("p a k -> p (a k)")), s)
                    for j in range(8):
                        has_u = not (last and j == 7)
                        has_k = not (last and j >= 6)
                        dve.wait_ge(gel_ready, tu + (j + 1))
                        nc.vector.tensor_tensor(wgt[:, j % 2, :], gel[:, j % 2, :], gate[:, j % 4, :],
                                                ALU.mult).then_inc(wgt_ready, 1)
                        steps = topk_steps(s, unit_src(t * 8 + (8 * t0 + j + 2)), None, (j + 2) % 4, tu + (j + 3),
                                           tu + (j + 3)) if has_k else []
                        if has_u:
                            dve.wait_ge(exp_gate, tu + (j + 2))
                            one(nc.vector.reciprocal(grcp, gsum[:, (j + 1) % 4:(j + 1) % 4 + 1]), s)
                            one(nc.vector.tensor_scalar(gate[:, (j + 1) % 4, :], gate[:, (j + 1) % 4, :], grcp, None,
                                                        ALU.mult), s)
                            if j == 7:
                                one(nc.vector.tensor_copy(h2cur, h2tok[:, bass.ds(t + (t0 + 1), 1), :]
                                                          .rearrange("p a d -> p (a d)")), s)
                            for k in range(16):
                                dot(k, k % 8, (j + 1) % 2, tu * 32 + (32 * (j + 1) + 16 * (k // 8 + 1)))
                                if k < len(steps):
                                    steps[k]()
                        assert len(steps) <= 16
                    dve.wait_ge(outT_done, t + (tile0 + 1))
                    for k in range(DK):
                        xx = X[:, k, bass.ds(t * P + t0 * P, P)]
                        nc.vector.scalar_tensor_tensor(out=xx, in0=banks[:, 2 + k // 4, (k % 4) * P:(k % 4 + 1) * P],
                                                       scalar=g2cur[:, k:k + 1], in1=xx, op0=ALU.mult,
                                                       op1=ALU.add).then_inc(outT_added, 1)
                    dve.wait_ge(outT_added, t * DK + (tile0 * DK + DK))

                s = [0, chain[0]]
                peer_tile(0, nt == 1, s)
                per_tile = s[0]
                chain[0] += per_tile
                if nt > 2:
                    with dve.Fori(1, nt - 1) as t:
                        s = [0, (t - 1) * per_tile + chain[0]]
                        peer_tile(t, False, s)
                        assert s[0] == per_tile
                    chain[0] += (nt - 2) * per_tile
                s = [0, chain[0]]
                peer_tile(nt - 1, True, s)
                chain[0] += s[0]
                dve.sem_inc(x_ready, 1)
                barrier(dve, stage_no(l, 6))

        @block.gpsimd
        def _(pool):
            pool.memset(epsc[:, :], EPS).then_inc(eps_ready, 1)
            pool.wait_ge(const_in, 16)

            def bias_head(l, h):
                if h >= 2:
                    b, use = jobs[(l, "na", h - 2, NBLK - 1, "s", 0)]
                    pool.wait_ge(bank_free[b], use + 1)
                pool.dma_start(bias[:, h % 2, :, 0:NLOC], na_bias[l, h]).then_inc(bias_in, 16)
                pool.wait_ge(bias_in, 16 * (HEADS * l + h + 1))
                bb = bias[:, h % 2, :, 0:NLOC].rearrange("p y (r j) -> p y r j", r=ROWS)
                mm = masks.rearrange("p (y j) -> p y j", y=3).unsqueeze(2).broadcast_to([P, 3, ROWS, KEY_COLS])
                pool.tensor_tensor(bb, bb, mm, ALU.add).then_inc(bias_ready, 1)

            for l in range(LAYERS):
                b, use = jobs[(l, "n1", CTX)]
                pool.wait_ge(bank_full[b], use + 1)
                pool.memset(bias[:, :, :, NLOC:512], 0.0).then_inc(bias_zero, 1)
                pool.wait_ge(bias_zero, l + 1)
                bias_head(l, 0)
                bias_head(l, 1)
                pool.wait_ge(v_copied, l + 1)
                for n in range(NBLK):
                    start = min(max(n * COL_BLK - WIN_C // 2, 0), GRID_W - KEY_COLS)
                    for cch in range(2):
                        for r in range(4):
                            row = 4 * cch + r
                            p0 = (row % 2) * GRID_W + start
                            pool.dma_start(vblk[32 * r:32 * r + 32, n, cch, :],
                                           vna[p0:p0 + 32, 2 + row // 2, :]).then_inc(vblk_in, 16)
                for h in range(2, HEADS):
                    bias_head(l, h)
                barrier(pool, stage_no(l, 1))
                pool.wait_ge(rope_done, 9 * l + 1)
                for hh in range(4):
                    pool.tensor_copy(km[64:96, hh, :], krT[64:96, :]).then_inc(kr_copied, 1)
                barrier(pool, stage_no(l, 2))
                pool.dma_start(bsb, sg_b[l:l + 1].rearrange("l g q -> l (g q)").broadcast_to([P, GROUPS * P])
                               .rearrange("p (g q) -> p g q", g=GROUPS)).then_inc(bsb_in, 16)
                pool.wait_ge(bsb_in, 16 * (l + 1))
                for k in (3, 4, 5):
                    barrier(pool, stage_no(l, k))
                t0, t1 = PEER_TILES(l)
                nt = t1 - t0
                unit0 = 0 if l == 0 else 48

                def gather(table, buf, sems, slot, col):
                    pool.indirect_dma_start(buf[:, slot, :], None, table,
                                            bass.IndirectOffsetOnAxis(ap=col, axis=0)).then_inc(sems[slot], 16)

                pool.wait_ge(idx_ready, unit0 + 1)
                for k in range(16):
                    if k >= U_RING or unit0:
                        pool.wait_ge(u_used, unit0 * 16 + k - U_RING + 1)
                    gather(u_rows, ub, u_full, k % U_RING, idx[:, 0, k:k + 1])

                def peer_tile(t, last, first):
                    for j in range(8):
                        for k in range(16):
                            g = j * 16 + k
                            if not (last and j == 7):
                                if k == 0:
                                    pool.wait_ge(idx_ready, t * 8 + (unit0 + j + 2))
                                    pool.sem_inc(pool_go, 1)
                                pool.wait_ge(u_used, t * 128 + (unit0 * 16 + g + 16 - U_RING + 1))
                                pool.sem_inc(pool_go, 1)
                                gather(u_rows, ub, u_full, k % U_RING, idx[:, (j + 1) % 4, k:k + 1])
                            if not (first and g < V_RING and not unit0):
                                pool.wait_ge(v_used, t * 128 + (unit0 * 16 + g - V_RING + 1))
                                pool.sem_inc(pool_go, 1)
                            gather(v_rows, vb, v_full, k % V_RING, idx[:, j % 4, k:k + 1])

                peer_tile(0, nt == 1, True)
                if nt > 2:
                    with pool.Fori(1, nt - 1) as t:
                        peer_tile(t, False, False)
                peer_tile(nt - 1, True, False)
                barrier(pool, stage_no(l, 6))

        @block.sync
        def _(sp):
            sp.dma_start(consts[:, :], const).then_inc(const_in, 16)
            sp.dma_start(cT[:, :, :], cond).then_inc(c_in, 16)

            def weights(n):
                name, parts = loads[n]
                s = n % W_SLOTS
                if n >= W_SLOTS:
                    b, use = jobs[last_use[loads[n - W_SLOTS][0]]]
                    sp.wait_ge(bank_full[b], use + 1)
                for off, src in parts:
                    shape = src.shape
                    if len(shape) == 3:
                        dst = wring[:, s, off:off + shape[1] * shape[2]].rearrange("p (k n) -> p k n", k=shape[1])
                    else:
                        dst = wring[:, s, off:off + shape[1]]
                    sp.dma_start(dst, src).then_inc(w_full[s], 16)

            sp.dma_start(smalls[:, :, :], columns).then_inc(small_in, 16)
            sp.dma_start(X[:, :, 0:CTX], ctx_in).then_inc(x_in, 16)
            sp.dma_start(X[:, :, CTX:T], x).then_inc(x_in, 16)
            for n in range(len(loads)):
                weights(n)
            sp.wait_ge(x_ready, 2 * LAYERS)
            sp.dma_start(out, X[:, :, CTX:T]).then_inc(out_in, 16)
            sp.wait_ge(out_in, 16)


_NAMES = ['x', 'ctx', 'na_rpb', 'sg_w', 'sg_b', 'mla_w_uk', 'mla_w_uv', 'peer_k1', 'peer_k2', 'peer_u', 'peer_v']


def tiled(w, cols):
    w = np.asarray(w)
    lead, (k, n) = w.shape[:-2], w.shape[-2:]
    a = w.reshape(lead + (k // P, P, n // cols, cols))
    z = len(lead)
    a = a.transpose(tuple(range(z)) + (z + 2, z + 1, z, z + 3))
    return a.reshape(lead + (n // cols, P, (k // P) * cols))


def bias_layout(rpb):
    pad = np.pad(np.asarray(rpb), ((0, 0), (0, 0), (0, 0), (16, 16)))
    q, k = np.arange(P), np.arange(NLOC)
    row = (k // KEY_COLS)[None, :] - (q // COL_BLK)[:, None] + WIN_R - 1
    col = (k % KEY_COLS)[None, :] - (q % COL_BLK)[:, None] + 16
    return np.stack([pad[:, :, row, col + s] for s in BIAS_SHIFT], axis=3)


def as_columns(inputs):
    def chunks(name):
        a = np.asarray(inputs[name])
        return a.reshape(LAYERS, -1, P).transpose(0, 2, 1)

    def stacked(*names):
        rows = [np.asarray(inputs[n]) if n else np.zeros((LAYERS, 64), np.float32) for n in names]
        a = np.concatenate(rows, axis=1)
        return np.pad(a, ((0, 0), (0, P - a.shape[1])))[:, :, None]

    return np.concatenate([chunks('b_mod'), chunks('g_norm1'), chunks('g_norm2'), stacked('na_g_q', 'na_g_q'),
                           stacked('na_g_k', 'na_g_k'), chunks('sg_g'), chunks('mla_g_cq'), chunks('mla_g_ckv'),
                           stacked('mla_g_qn', 'mla_g_qr'), stacked('mla_g_kn'), stacked(None, 'mla_g_kr'),
                           np.zeros((LAYERS, P, 4), np.float32)], axis=2)


def kernel(**inputs):
    import numpy as _np
    import concourse.bacc as _bacc
    from concourse import mybir as _mybir
    from concourse.bass_utils import run_bass_kernel_spmd as _run

    nc = _bacc.Bacc("TRN2", target_bir_lowering=False, num_devices=1)
    arrays, args = {}, []

    def feed(name, a):
        a = _np.ascontiguousarray(a)
        arrays[name] = a
        args.append(nc.dram_tensor(name, a.shape, _mybir.dt.from_np(a.dtype), kind="ExternalInput").ap())

    for name in _NAMES:
        a = _np.asarray(inputs[name])
        if name == "na_rpb":
            a = bias_layout(a)
        if name in ("x", "ctx"):
            a = a[0].T.reshape(D // P, P, -1).transpose(1, 0, 2)
        feed(f"in_{name}_dram", a)
    w_in = _np.asarray(inputs['w_in'])
    feed("w_mod_dram", tiled(inputs['w_mod'], 256))
    for part, c0, c1, cols in (("qkv", C_V, C_CQ, 256), ("cq", C_CQ, C_CKV, 256), ("ckv", C_CKV, C_U, 160),
                               ("uq", None, None, 768), ("sg", C_U, C_GATE, 256), ("gate", C_GATE, C_GATE + 3 * D, 256)):
        if part == "uq":
            feed("w_uq_dram", tiled(inputs['mla_w_uq'], cols))
        elif part == "qkv":
            feed("w_qkv_dram", tiled(_np.concatenate([w_in[:, :, C_V:C_CQ], w_in[:, :, C_Q:C_V]], axis=2), cols))
        else:
            feed(f"w_{part}_dram", tiled(w_in[:, :, c0:c1], cols))
    feed("w_branch_dram", tiled(inputs['w_branch'], 512))
    feed("w_out_dram", tiled(inputs['w_out'], 256))
    feed("peer_w_q_dram", tiled(inputs['peer_w_q'], 256))
    pair = _np.stack([_np.asarray(inputs['c'])[0], _np.asarray(inputs['c_ctx'])], axis=-1)
    feed("cond_dram", pair.reshape(D // P, P, 2).transpose(1, 0, 2))
    feed("columns_dram", as_columns(inputs).transpose(1, 0, 2))
    feed("const_dram", constants())
    args.append(nc.dram_tensor("out_0_dram", (P, D // P, SEQ), _mybir.dt.float32, kind="ExternalOutput").ap())
    program(nc, *args)
    r = _run(nc, [arrays], core_ids=[0])
    o = r.results[0]["out_0_dram"]
    return o.transpose(2, 1, 0).reshape(1, SEQ, D)
```
